# Optimizing a Trainium2 kernel written in Bass

```python
import jax, jax.numpy as jnp
from jax import lax
import numpy as np

D_MODEL = 1024
BATCH = 1
SEQ = 256
DEPTH = 2

HEAD_DIM = 64
N_GROUPS_A = 4
N_HEADS_B = 6
N_HEADS_C = 6
W_A = N_GROUPS_A * HEAD_DIM
W_B = N_HEADS_B * HEAD_DIM
W_C = N_HEADS_C * HEAD_DIM
D_MIX = W_A + W_B + W_C
OFF_B = W_A
OFF_C = W_A + 2 * W_B
D_IN_PROJ = W_A + 2 * W_B + 3 * W_C
CHUNK = 128
CONV_WIDTH = 3
D_FF_DENSE = 2816
N_EXPERTS = 8
TOP_K = 2
D_FF_EXPERT = 3584
N_DENSE = (DEPTH + 1) // 2
N_MOE = DEPTH // 2
EPS = 1e-6

kernel_name = "hybrid_fourier_gmlp_shortconv_moe_encoder"

def rmsnorm(x, g):
    x32 = x.astype(jnp.float32)
    y = x32 * lax.rsqrt(jnp.mean(x32 * x32, axis=-1, keepdims=True) + EPS)
    return (y * g.astype(jnp.float32)).astype(x.dtype)

def layernorm(x, g, b):
    x32 = x.astype(jnp.float32)
    mu = jnp.mean(x32, axis=-1, keepdims=True)
    xc = x32 - mu
    y = xc * lax.rsqrt(jnp.mean(xc * xc, axis=-1, keepdims=True) + EPS)
    return (y * g.astype(jnp.float32) + b.astype(jnp.float32)).astype(x.dtype)

def depthwise_conv_centred(x, w):
    c = x.shape[-1]
    return lax.conv_general_dilated(
        x, w[:, None, :].astype(x.dtype), window_strides=(1,),
        padding=((CONV_WIDTH // 2, CONV_WIDTH // 2),),
        dimension_numbers=('NWC', 'WIO', 'NWC'), feature_group_count=c)

def hybrid_mixer(h, w_in, vg, vb, ws, bs, cw, w_out):
    bn, s, _ = h.shape
    p = h @ w_in
    a = p[..., :W_A].reshape(bn, s, N_GROUPS_A, HEAD_DIM).astype(jnp.float32)
    a = jnp.fft.fftn(a, axes=(1, 3), norm='ortho').real
    a = a.reshape(bn, s, W_A).astype(h.dtype)
    uv = jax.nn.gelu(p[..., OFF_B:OFF_C])
    u, v = uv[..., :W_B], uv[..., W_B:]
    v = layernorm(v, vg, vb).reshape(bn, s // CHUNK, CHUNK, N_HEADS_B, HEAD_DIM)
    z = jnp.einsum('hpq,bcqhd->bcphd', ws, v) + bs[None, None, :, :, None]
    g = u * z.reshape(bn, s, W_B)
    pc = p[..., OFF_C:]
    b_gate, c_gate, xc = pc[..., :W_C], pc[..., W_C:2 * W_C], pc[..., 2 * W_C:]
    y = b_gate * depthwise_conv_centred(c_gate * xc, cw)
    return jnp.concatenate([a, g, y], axis=-1) @ w_out

def swiglu(h, wg, wu, wd):
    return (jax.nn.silu(h @ wg) * (h @ wu)) @ wd

def moe_swiglu(h, router_w, wg, wu, wd):
    logits = (h @ router_w).astype(jnp.float32)
    top_v, top_i = lax.top_k(logits, TOP_K)
    gates = jax.nn.softmax(top_v, axis=-1)
    combine = jnp.sum(jax.nn.one_hot(top_i, N_EXPERTS, dtype=jnp.float32) * gates[..., None], axis=-2)
    combine = combine.astype(h.dtype)
    out = jnp.zeros_like(h)
    for e in range(N_EXPERTS):
        out = out + combine[..., e:e + 1] * swiglu(h, wg[e], wu[e], wd[e])
    return out

def setup_inputs(seed: int = 0) -> dict:
    key = jax.random.key(seed)
    ks = jax.random.split(key, 20)
    f32 = jnp.float32
    nrm = lambda k, shape, scale: jax.random.normal(k, shape, f32) * scale
    return {
        'x': nrm(ks[0], (BATCH, SEQ, D_MODEL), 1.0),
        'norm_mix_g': 1.0 + nrm(ks[1], (DEPTH, D_MODEL), 0.01),
        'w_in': nrm(ks[2], (DEPTH, D_MODEL, D_IN_PROJ), D_MODEL ** -0.5),
        'vnorm_g': 1.0 + nrm(ks[3], (DEPTH, W_B), 0.01),
        'vnorm_b': nrm(ks[4], (DEPTH, W_B), 0.01),
        'w_spatial': nrm(ks[5], (DEPTH, N_HEADS_B, CHUNK, CHUNK), CHUNK ** -0.5),
        'b_spatial': 1.0 + nrm(ks[6], (DEPTH, CHUNK, N_HEADS_B), 0.01),
        'conv_w': nrm(ks[7], (DEPTH, CONV_WIDTH, W_C), CONV_WIDTH ** -0.5),
        'w_out': nrm(ks[8], (DEPTH, D_MIX, D_MODEL), D_MIX ** -0.5),
        'norm_ffn_g': 1.0 + nrm(ks[9], (DEPTH, D_MODEL), 0.01),
        'dense_w_gate': nrm(ks[10], (N_DENSE, D_MODEL, D_FF_DENSE), D_MODEL ** -0.5),
        'dense_w_up': nrm(ks[11], (N_DENSE, D_MODEL, D_FF_DENSE), D_MODEL ** -0.5),
        'dense_w_down': nrm(ks[12], (N_DENSE, D_FF_DENSE, D_MODEL), D_FF_DENSE ** -0.5),
        'router_w': nrm(ks[13], (N_MOE, D_MODEL, N_EXPERTS), D_MODEL ** -0.5),
        'moe_w_gate': nrm(ks[14], (N_MOE, N_EXPERTS, D_MODEL, D_FF_EXPERT), D_MODEL ** -0.5),
        'moe_w_up': nrm(ks[15], (N_MOE, N_EXPERTS, D_MODEL, D_FF_EXPERT), D_MODEL ** -0.5),
        'moe_w_down': nrm(ks[16], (N_MOE, N_EXPERTS, D_FF_EXPERT, D_MODEL), D_FF_EXPERT ** -0.5),
        'norm_final_g': 1.0 + nrm(ks[17], (D_MODEL,), 0.01),
    }

def reference(x, norm_mix_g, w_in, vnorm_g, vnorm_b, w_spatial, b_spatial, conv_w, w_out,
              norm_ffn_g, dense_w_gate, dense_w_up, dense_w_down, router_w,
              moe_w_gate, moe_w_up, moe_w_down, norm_final_g):
    h = x
    for i in range(DEPTH):
        hn = rmsnorm(h, norm_mix_g[i])
        h = h + hybrid_mixer(hn, w_in[i], vnorm_g[i], vnorm_b[i], w_spatial[i],
                             b_spatial[i], conv_w[i], w_out[i])
        hn = rmsnorm(h, norm_ffn_g[i])
        j = i // 2
        if i % 2 == 0:
            h = h + swiglu(hn, dense_w_gate[j], dense_w_up[j], dense_w_down[j])
        else:
            h = h + moe_swiglu(hn, router_w[j], moe_w_gate[j], moe_w_up[j], moe_w_down[j])
    return rmsnorm(h, norm_final_g)


_drawn_inputs = setup_inputs


def setup_inputs(seed=0):
    import zlib

    import numpy as np

    out = dict(_drawn_inputs(seed))
    spreads = {}
    factors = {'vnorm_g': 22.732,
     'vnorm_b': 27.407,
     'b_spatial': 18.722,
     'norm_final_g': 32.866,
     'norm_mix_g': 2.68,
     'norm_ffn_g': 8.0}
    for name, (base, spread) in spreads.items():
        noise = np.random.default_rng([zlib.crc32(name.encode()), seed]).standard_normal(out[name].shape)
        drawn = base * np.exp(spread * noise) if base else spread * noise
        out[name] = __import__('jax').numpy.asarray(drawn.astype(out[name].dtype))
    for name, factor in factors.items():
        out[name] = (out[name] * factor).astype(out[name].dtype)
    return out
```

```python
import numpy as np

import concourse.bass as bass
from concourse import mybir
from contextlib import ExitStack

F32 = mybir.dt.float32
F32R = mybir.dt.float32r
I32 = mybir.dt.int32
U32 = mybir.dt.uint32
ALU = mybir.AluOpType
ACT = mybir.ActivationFunctionType
AX = mybir.AxisListType

P = 128
BANK = 512
EPS = 1e-6
TOP_K = 2
GROUPS_A = 4


def hybrid_encoder(nc, x, norm_mix_g, w_in, vnorm_g, vnorm_b, w_spatial, b_spatial, conv_w, w_out,
                   norm_ffn_g, dense_w_gate, dense_w_up, dense_w_down, router_w,
                   moe_w_gate, moe_w_up, moe_w_down, norm_final_g, dft_seq, dft_head, out):
    _, SEQ, D = x.shape
    DEPTH, _, D_IN = w_in.shape
    W_B = vnorm_g.shape[1]
    HEADS_B = b_spatial.shape[2]
    HEAD = W_B // HEADS_B
    TAPS, W_C = conv_w.shape[1:]
    W_A = D_IN - 2 * W_B - 3 * W_C
    F_DENSE = dense_w_gate.shape[2]
    E = router_w.shape[2]
    F_EXP = moe_w_gate.shape[3]
    NT = SEQ // P
    KT = D // P
    TOKEN_COLS = W_A + 2 * W_B
    FEAT_TILES = 3 * W_C // P
    CT = W_C // P
    AT = W_A // P
    BT = W_B // P
    assert NT == 2 and KT == 8 and TOKEN_COLS == 2 * BANK and SEQ == 2 * P and E == 8

    SLOT = 2048
    RAW = 6
    SPLIT = 3
    MIX_IN_TOKEN = 4
    MIX_IN_FEAT = -(-FEAT_TILES // 2)
    MIX_IN = MIX_IN_TOKEN + MIX_IN_FEAT
    MIX_OUT = KT // 2
    MIX_SLOTS = MIX_IN + MIX_OUT
    DENSE_STEPS = F_DENSE // (2 * P)
    DENSE_SLOTS = 3 * DENSE_STEPS
    CHUNKS = F_EXP // BANK
    ITEM = 6 * CHUNKS
    MIX_BASE = [0, MIX_SLOTS + DENSE_SLOTS]
    DENSE_BASE = MIX_SLOTS
    MOE_BASE = 2 * MIX_SLOTS + DENSE_SLOTS
    assert ITEM % RAW == 0 and ITEM % SPLIT == 0 and DENSE_STEPS % 2 == 1

    OVER = (TOP_K * SEQ) // (P + 1)
    ITEMS = E + OVER
    TAB = 8
    RANK, SEL, GATE, EID = 0, 2, 4, 6
    RES_BASE = 3 * 4

    ctx = ExitStack()
    with ctx:
        def sb(name, shape, dt=F32):
            return ctx.enter_context(nc.sbuf_tensor(name, shape, dt))

        def sem(name):
            return ctx.enter_context(nc.semaphore(name))

        raw = sb("raw", [P, RAW, SLOT])
        w_hi = sb("w_hi", [P, SPLIT, SLOT], F32R)
        w_lo = sb("w_lo", [P, SPLIT, SLOT], F32R)
        h = sb("h", [P, NT, D])
        hn = sb("hn", [P, NT, D])
        xT_hi = sb("xT_hi", [P, KT, SEQ], F32R)
        xT_lo = sb("xT_lo", [P, KT, SEQ], F32R)
        mix_hi = sb("mix_hi", [P, KT * SEQ], F32R)
        mix_lo = sb("mix_lo", [P, KT * SEQ], F32R)
        mixT_hi = mix_hi[:, :].rearrange("p (k s) -> p k s", k=KT)
        mixT_lo = mix_lo[:, :].rearrange("p (k s) -> p k s", k=KT)
        hn_hi = mix_hi[:, :].rearrange("p (t d) -> p t d", t=NT)
        hn_lo = mix_lo[:, :].rearrange("p (t d) -> p t d", t=NT)
        a_sb = sb("a_sb", [P, NT, W_A])
        uv = sb("uv", [P, NT * 2 * W_B])
        uv_t = uv[:, :].rearrange("p (t c) -> p t c", t=NT)
        ws_raw = uv[:, 0:DEPTH * HEADS_B * P].rearrange("p (h q) -> p h q", q=P)
        wsT = sb("wsT", [P, DEPTH * HEADS_B, P])
        featT = sb("featT", [P, 2 * MIX_IN_FEAT * SEQ])
        feat = featT[:, :].rearrange("p (f s) -> p f s", s=SEQ)
        dft1 = sb("dft1", [P, AT * BANK])
        dft1_g = dft1[:, :].rearrange("p (g c) -> p g c", g=AT)
        y_sb = dft1
        pad = sb("pad", [P, CT, SEQ + 2])
        cs = sb("cs", [P, NT, 2 * SEQ])
        bd = sb("bd", [P, 2, P])
        ident = sb("ident", [P, P])
        before = sb("before", [P, P])
        ones = sb("ones", [P, P])
        iota = sb("iota", [P, P])
        g_bc = sb("g_bc", [P, 2, D])
        vg_bc = sb("vg_bc", [P, DEPTH, W_B])
        vb_bc = sb("vb_bc", [P, DEPTH, W_B])
        bs = sb("bs", [P, DEPTH, HEADS_B])
        cw = sb("cw", [P, DEPTH, TAPS * CT])
        rw = sb("rw", [P, KT, E])
        rw_hi = sb("rw_hi", [P, KT, E], F32R)
        rw_lo = sb("rw_lo", [P, KT, E], F32R)
        sg = sb("sg", [P, BANK])
        hmul = sb("hmul", [P, BANK])
        hT_hi = sb("hT_hi", [P, BANK], F32R)
        hT_lo = sb("hT_lo", [P, BANK], F32R)
        pick = sb("pick", [P, NT, P], F32R)
        pg = featT[:, 0:NT * P].rearrange("p (t s) -> p t s", t=NT)
        pgT = featT[:, NT * P:2 * NT * P].rearrange("p (t s) -> p t s", t=NT)
        tab = sb("tab", [P, ITEMS + 2, TAB])
        cur = sb("cur", [P, 2, TAB])
        stat = sb("stat", [P, 4, 2 * (DEPTH * 2 + 1)])
        bn = sb("bn", [P, DEPTH * NT, 6])
        mv = sb("mv", [P, DEPTH * NT, 2])
        vst = sb("vst", [P, 3, DEPTH * NT])
        eps_c = sb("eps_c", [P, 1])
        lg = sb("lg", [P, NT, E])
        top = sb("top", [P, NT, E])
        topi = sb("topi", [P, NT, E], U32)
        topf = sb("topf", [P, NT, E])
        rt = sb("rt", [P, 4, NT])
        oh = sb("oh", [P, 2 * NT, E])
        sel = sb("sel", [P, NT, E])
        over = sb("over", [P, 2, E])
        ohj = sb("ohj", [P, OVER, E])
        prod = sb("prod", [P, TAB, E])
        steer = sb("steer", [1, OVER + 2], I32)

        banks = [ctx.enter_context(nc.psum_tensor(n, [P, BANK], F32))
                 for n in ("pG", "pU", "pY0", "pY1", "pS0", "pS1", "pS2", "pS3")]
        pG, pU, pY0, pY1, *pS = banks
        pY = [pY0, pY1]
        FEAT_BANK = [pG, pU, pY0, pY1, pG]
        OUT_BANK = [pS[2], pS[3], pU, pY0]

        slot_loaded = [sem(f"slot_loaded{i}") for i in range(RAW)]
        hi_ready, lo_ready, slots_used = sem("hi_ready"), sem("lo_ready"), sem("slots_used")
        x_loaded = [sem(f"x_loaded{t}") for t in range(NT)]
        ws_loaded, dft_loaded, row_loaded, rw_loaded = (sem("ws_loaded"), sem("dft_loaded"),
                                                        sem("row_loaded"), sem("rw_loaded"))
        g_loaded = [sem(f"g_loaded{i}") for i in range(2)]
        masks_set, masks_ready = sem("masks_set"), sem("masks_ready")
        ws_turned, wsT_ready = sem("ws_turned"), sem("wsT_ready")
        sq_ready, ms_ready, root_ready, inv_ready, hn_ready = (sem("sq_ready"), sem("ms_ready"), sem("root_ready"),
                                                               sem("inv_ready"), sem("hn_ready"))
        hn_turned, xhi_ready, xlo_ready = sem("hn_turned"), sem("xhi_ready"), sem("xlo_ready")
        a_ready, uv_ready, feat_ready = sem("a_ready"), sem("uv_ready"), sem("feat_ready")
        dft1_done, dft1_ready, dft2_done = sem("dft1_done"), sem("dft1_ready"), sem("dft2_done")
        ln_step, ln_root, vn_ready = sem("ln_step"), sem("ln_root"), sem("vn_ready")
        z_done, g_ready, g_turned = sem("z_done"), sem("g_ready"), sem("g_turned")
        conv_step, y_ready = sem("conv_step"), sem("y_ready")
        mixhi_ready, mixlo_ready = sem("mixhi_ready"), sem("mixlo_ready")
        res_added = sem("res_added")
        silu_ready, hmul_ready, h_turned, hhi_ready, hlo_ready = (sem("silu_ready"), sem("hmul_ready"), sem("h_turned"),
                                                                  sem("hhi_ready"), sem("hlo_ready"))
        rwhi_ready, rwlo_ready, logits_done = sem("rwhi_ready"), sem("rwlo_ready"), sem("logits_done")
        hnhi_ready, hnlo_ready = sem("hnhi_ready"), sem("hnlo_ready")
        route_step, diff_ready, exp_ready, sel_ready, ranks_done, table_ready, steer_ready = (
            sem("route_step"), sem("diff_ready"), sem("exp_ready"), sem("sel_ready"), sem("ranks_done"),
            sem("table_ready"), sem("steer_ready"))
        cur_ready, pick_ready, pg_ready, pg_turned, pgT_ready = (sem("cur_ready"), sem("pick_ready"), sem("pg_ready"),
                                                                 sem("pg_turned"), sem("pgT_ready"))
        gathered, gxhi_ready, gxlo_ready = sem("gathered"), sem("gxhi_ready"), sem("gxlo_ready")
        y_copied, scattered, stored = sem("y_copied"), sem("scattered"), sem("stored")

        block = ctx.enter_context(nc.Block())

        def four_k(s):
            return s.rearrange("p (k n) -> p k n", n=BANK)

        def eight_k(s, n=2 * P):
            return s[:, 0:KT * n].rearrange("p (k n) -> p k n", n=n)

        def two_k(s):
            return s.rearrange("p (k n) -> p k n", n=D)

        def slot_hi(n):
            return w_hi[:, n % SPLIT, :]

        def slot_lo(n):
            return w_lo[:, n % SPLIT, :]

        def chunk_slot(c):
            return 6 * c - 2 if c else 0

        @block.sync
        def _(sp):
            for t in range(NT):
                sp.dma_start(h[:, t, :], x[0, t * P:(t + 1) * P, :]).then_inc(x_loaded[t], 16)

            def load(n, view, src, it=0, per=ITEM):
                if n >= RAW:
                    sp.wait_ge(lo_ready, n - RAW + 1 + per * it)
                sp.dma_start(view(raw[:, n % RAW, :]), src).then_inc(slot_loaded[n % RAW], 16)

            def mix_loads(layer):
                b = MIX_BASE[layer]
                w = w_in[layer].rearrange("(k p) n -> p k n", p=P)
                for i in range(MIX_IN_TOKEN):
                    j, kh = i // 2, i % 2
                    load(b + i, four_k, w[:, 4 * kh:4 * kh + 4, j * BANK:(j + 1) * BANK])
                for i in range(MIX_IN_FEAT):
                    c0 = TOKEN_COLS + 2 * P * i
                    n = min(2 * P, D_IN - c0)
                    load(b + MIX_IN_TOKEN + i, lambda s: eight_k(s, n), w[:, :, c0:c0 + n])
                w = w_out[layer].rearrange("(k p) n -> p k n", p=P)
                for i in range(MIX_OUT):
                    load(b + MIX_IN + i, two_k, w[:, 2 * i:2 * i + 2, :])

            def dense_load(n, w, s, rounds=0):
                if w is dense_w_down:
                    view, src = two_k, w[0].rearrange("(f p) n -> p f n", p=P)[:, bass.ds(2 * s, 2), :]
                else:
                    view, src = eight_k, w[0].rearrange("(k p) n -> p k n", p=P)[:, :, bass.ds(2 * P * s, 2 * P)]
                load(n, view, src, rounds, RAW)

            mix_loads(0)
            dense_load(DENSE_BASE, dense_w_gate, 0)
            dense_load(DENSE_BASE + 1, dense_w_up, 0)
            with sp.Fori(0, DENSE_STEPS // 2) as r:
                for u in range(2):
                    n0 = DENSE_BASE + 2 + 3 * u
                    dense_load(n0, dense_w_gate, 2 * r + 1 + u, r)
                    dense_load(n0 + 1, dense_w_up, 2 * r + 1 + u, r)
                    dense_load(n0 + 2, dense_w_down, 2 * r + u, r)
            dense_load(DENSE_BASE + DENSE_SLOTS - 1, dense_w_down, DENSE_STEPS - 1)
            mix_loads(1)

            def item_load(i, expert, it):
                c = 0 if i < 4 else (i + 2) // 6
                k = i - chunk_slot(c)
                if i >= chunk_slot(CHUNKS):
                    c, k = CHUNKS, i - chunk_slot(CHUNKS) + 4
                if k < 4:
                    w = moe_w_gate if k < 2 else moe_w_up
                    src = w[0, bass.ds(expert, 1), (k % 2) * D // 2:(k % 2 + 1) * D // 2, c * BANK:(c + 1) * BANK]
                    load(MOE_BASE + i, four_k, src.rearrange("o (k p) n -> p (o k) n", p=P), it)
                else:
                    f0 = (c - 1) * BANK + (k - 4) * 2 * P
                    src = moe_w_down[0, bass.ds(expert, 1), f0:f0 + 2 * P, :]
                    load(MOE_BASE + i, two_k, src.rearrange("o (f p) n -> p (o f) n", p=P), it)

            with sp.Fori(0, E) as it:
                for i in range(ITEM):
                    item_load(i, it, it)
            sp.wait_ge(steer_ready, 2)
            extra = sp.value_load(steer[0:1, OVER + 1:OVER + 2], min_val=0, max_val=OVER)
            first = sp.value_load(steer[0:1, 0:1], min_val=0, max_val=E - 1)
            for i in range(2):
                item_load(i, first, E)
            with sp.Fori(0, OVER) as j:
                with sp.If(extra > j):
                    mine = sp.value_load(steer[0:1, bass.ds(j, 1)], min_val=0, max_val=E - 1)
                    for i in range(2, ITEM):
                        item_load(i, mine, j + E)
                    following = sp.value_load(steer[0:1, bass.ds(j + 1, 1)], min_val=0, max_val=E - 1)
                    for i in range(2):
                        item_load(i, following, j + E + 1)
            for t in range(NT):
                sp.wait_ge(hn_ready, 2 * 2 * DEPTH + t + 1)
                sp.dma_start(out[0, t * P:(t + 1) * P, :], hn[:, t, :]).then_inc(stored, 16)
            sp.wait_ge(stored, 16 * NT)

        @block.gpsimd
        def _(pool):
            gains = [norm_mix_g[0:1, :], norm_ffn_g[0:1, :], norm_mix_g[1:2, :], norm_ffn_g[1:2, :],
                     norm_final_g.rearrange("(o n) -> o n", o=1)]

            def load_gain(m):
                pool.dma_start(g_bc[:, m % 2, :], gains[m].to_broadcast([P, D])).then_inc(g_loaded[m % 2], 16)

            pool.memset(ident[:, :], 0.0).then_inc(masks_set, 1)
            pool.wait_ge(masks_set, 1)
            pool.affine_select(out=ident[:, :], in_=ident[:, :], compare_op=ALU.not_equal, fill=1.0, base=0,
                               pattern=[[-1, P]], channel_multiplier=1).then_inc(masks_ready, 1)
            load_gain(0)
            load_gain(1)
            pool.memset(ones[:, :], 1.0).then_inc(masks_set, 1)
            pool.wait_ge(masks_set, 2)
            pool.affine_select(out=before[:, :], in_=ones[:, :], compare_op=ALU.is_gt, fill=0.0, base=0,
                               pattern=[[1, P]], channel_multiplier=-1).then_inc(masks_ready, 1)
            pool.memset(eps_c[:, :], EPS).then_inc(masks_ready, 1)
            pool.memset(pad[:, :, 0:1], 0.0).then_inc(masks_ready, 1)
            pool.memset(pad[:, :, SEQ + 1:SEQ + 2], 0.0).then_inc(masks_ready, 1)
            pool.iota(iota[:, :], pattern=[[1, P]], base=0, channel_multiplier=0,
                      allow_small_or_imprecise_dtypes=True).then_inc(masks_ready, 1)
            pool.memset(tab[:, :, :], 0.0).then_inc(masks_ready, 1)
            for m in range(2, len(gains)):
                pool.wait_ge(hn_ready, 2 * (m - 2) + 2)
                load_gain(m)

        MASKS = 7

        @block.scalar
        def _(act):
            act.dma_start(ws_raw, w_spatial.rearrange("l h p q -> p (l h) q")).then_inc(ws_loaded, 16)
            act.dma_start(cs[:, :, :], dft_seq.rearrange("(t p) n -> p t n", p=P)).then_inc(dft_loaded, 16)
            act.dma_start(bd[:, :, :], dft_head.rearrange("c p n -> p c n")).then_inc(dft_loaded, 16)
            for layer in range(DEPTH):
                act.dma_start(vg_bc[:, layer, :], vnorm_g[layer:layer + 1, :].to_broadcast([P, W_B])) \
                    .then_inc(row_loaded, 16)
                act.dma_start(vb_bc[:, layer, :], vnorm_b[layer:layer + 1, :].to_broadcast([P, W_B])) \
                    .then_inc(row_loaded, 16)
                act.dma_start(bs[:, layer, :], b_spatial[layer]).then_inc(row_loaded, 16)
                for tap in range(TAPS):
                    act.dma_start(cw[:, layer, tap * CT:(tap + 1) * CT],
                                  conv_w[layer, tap, :].rearrange("(f p) -> p f", p=P),
                                  allow_slow_non_contiguous=True).then_inc(row_loaded, 16)
            act.dma_start(rw[:, :, :], router_w[0].rearrange("(k p) e -> p k e", p=P)).then_inc(rw_loaded, 16)

            def split(n, it=0, per=ITEM):
                rounds = per // RAW
                act.wait_ge(slot_loaded[n % RAW], 16 * (n // RAW + 1) + 16 * rounds * it)
                if n >= SPLIT:
                    act.wait_ge(slots_used, n - SPLIT + 1 + per * it)
                act.activation(slot_hi(n), raw[:, n % RAW, :], ACT.Copy).then_inc(hi_ready, 1)

            def split_half(n):
                act.wait_ge(slot_loaded[n % RAW], 16 * (n // RAW + 1))
                act.wait_ge(slots_used, n - SPLIT + 1)
                act.activation(slot_hi(n)[:, 0:KT * P], raw[:, n % RAW, 0:KT * P], ACT.Copy).then_inc(hi_ready, 1)

            def norm(m):
                for t in range(NT):
                    if m == 0:
                        act.wait_ge(x_loaded[t], 16)
                    else:
                        act.wait_ge(res_added, 4 * (m - 1) + 2 * (t + 1))
                    if m >= 1:
                        act.wait_ge(hn_ready, 2 * m)
                    act.activation(hn[:, t, :], h[:, t, :], ACT.Square,
                                   accum_out=stat[:, 0, 2 * m + t:2 * m + t + 1]).then_inc(sq_ready, 1)
                for t in range(NT):
                    act.wait_ge(ms_ready, 2 * m + t + 1)
                    act.activation(stat[:, 2, 2 * m + t:2 * m + t + 1], stat[:, 1, 2 * m + t:2 * m + t + 1],
                                   ACT.Sqrt).then_inc(root_ready, 1)
                for t in range(NT):
                    for q in range(2):
                        act.wait_ge(hn_turned, 4 * m + 2 * t + q + 1)
                        act.activation(xT_hi[:, 4 * q:4 * q + 4, t * P:(t + 1) * P],
                                       pS[2 * t + q][:, :].rearrange("p (k s) -> p k s", k=4),
                                       ACT.Copy).then_inc(xhi_ready, 1)

            def mix(layer):
                b = MIX_BASE[layer]
                f = b + MIX_IN_TOKEN
                norm(2 * layer)
                for n in range(b + 2, b + MIX_SLOTS + 2):
                    if n == f + MIX_IN_FEAT - 1:
                        split_half(n)
                    else:
                        split(n)
                    if n == b + 4:
                        act.wait_ge(slots_used, b + 2)
                        for t in range(NT):
                            act.activation(a_sb[:, t, :], pS[t][:, 0:W_A], ACT.Copy).then_inc(a_ready, 1)
                        if layer == 0:
                            act.wait_ge(wsT_ready, 1)
                        for t in range(NT):
                            act.activation(uv_t[:, t, 0:BANK - W_A], pS[t][:, W_A:BANK],
                                           ACT.Gelu_apprx_tanh).then_inc(uv_ready, 1)
                    if n == b + 6:
                        act.wait_ge(slots_used, b + 4)
                        for t in range(NT):
                            act.activation(uv_t[:, t, BANK - W_A:2 * W_B], pS[2 + t][:, :],
                                           ACT.Gelu_apprx_tanh).then_inc(uv_ready, 1)
                        for t in range(NT):
                            act.wait_ge(ln_step, 5 * (NT * layer + t) + 3)
                            k = NT * layer + t
                            act.activation(vst[:, 1, k:k + 1], vst[:, 0, k:k + 1], ACT.Sqrt).then_inc(ln_root, 1)
                    i = n - f - SPLIT
                    if 0 <= i < MIX_IN_FEAT:
                        act.wait_ge(slots_used, f + i + 1)
                        w = min(2, FEAT_TILES - 2 * i)
                        act.activation(feat[:, 2 * i:2 * i + w, :],
                                       FEAT_BANK[i][:, 0:w * SEQ].rearrange("p (f s) -> p f s", f=w),
                                       ACT.Copy).then_inc(feat_ready, 1)
                    if n == f + 4:
                        act.wait_ge(dft2_done, layer + 1)
                        act.activation(mixT_hi[:, 0:AT, :], pS[0][:, :].rearrange("p (k s) -> p k s", k=AT),
                                       ACT.Copy).then_inc(mixhi_ready, 1)
                    if n == f + 6:
                        act.wait_ge(g_turned, 2 * layer + 1)
                        act.activation(mixT_hi[:, AT:AT + 2, :], pS[1][:, :].rearrange("p (k s) -> p k s", k=2),
                                       ACT.Copy).then_inc(mixhi_ready, 1)
                        act.wait_ge(g_turned, 2 * layer + 2)
                        act.activation(mixT_hi[:, AT + 2, :], pS[0][:, 0:SEQ], ACT.Copy).then_inc(mixhi_ready, 1)
                    if n == b + 11:
                        for ft in range(CT):
                            act.wait_ge(y_ready, CT * layer + ft + 1)
                            act.activation(mixT_hi[:, AT + BT + ft, :], feat[:, ft, :],
                                           ACT.Copy).then_inc(mixhi_ready, 1)

            def dense_step(n0, s, rounds=0):
                it = dict(it=rounds, per=RAW)
                split(n0 + 2, **it)
                act.wait_ge(slots_used, n0 + 1 + RAW * rounds)
                act.wait_ge(hmul_ready, s + 2 * rounds)
                act.activation(sg[:, :], pG[:, :], ACT.Silu).then_inc(silu_ready, 1)
                split(n0 + 3, **it)
                split(n0 + 4, **it)
                act.wait_ge(hmul_ready, s + 1 + 2 * rounds)
                act.wait_ge(slots_used, n0 + 3 + RAW * rounds)
                act.activation(hT_hi[:, :], hmul[:, :], ACT.Copy).then_inc(hhi_ready, 1)

            def dense():
                norm(1)
                b = DENSE_BASE
                split(b + 2)
                act.wait_ge(slots_used, b + 1)
                act.activation(sg[:, :], pG[:, :], ACT.Silu).then_inc(silu_ready, 1)
                split(b + 3)
                act.wait_ge(hmul_ready, 1)
                act.activation(hT_hi[:, :], hmul[:, :], ACT.Copy).then_inc(hhi_ready, 1)
                with act.Fori(0, DENSE_STEPS // 2) as r:
                    for u in range(2):
                        dense_step(b + 2 + 3 * u, 1 + u, r)
                split(b + DENSE_SLOTS + 1)

            def evacuate_gather(g):
                for q in range(2):
                    act.wait_ge(gathered, 4 * g + q + 1)
                    act.activation(xT_hi[:, 4 * q:4 * q + 4, 0:P],
                                   pS[1 + q][:, :].rearrange("p (k s) -> p k s", k=4),
                                   ACT.Copy).then_inc(gxhi_ready, 1)

            def route():
                norm(3)
                act.wait_ge(rw_loaded, 16)
                act.activation(rw_hi[:, :, :], rw[:, :, :], ACT.Copy).then_inc(rwhi_ready, 1)
                for t in range(NT):
                    act.activation(hn_hi[:, t, :], hn[:, t, :], ACT.Copy).then_inc(hnhi_ready, 1)
                act.wait_ge(diff_ready, 1)
                act.activation(rt[:, 1, :], rt[:, 0, :], ACT.Exp).then_inc(exp_ready, 1)
                evacuate_gather(0)

            H0 = DENSE_STEPS

            def item(it):
                B = MOE_BASE
                for c in range(CHUNKS):
                    n0 = chunk_slot(c)
                    done = H0 + c + CHUNKS * it
                    split(B + n0 + 2, it)
                    if c >= 1:
                        act.wait_ge(h_turned, c + CHUNKS * it)
                        act.wait_ge(slots_used, B + n0 + ITEM * it)
                        act.activation(hT_hi[:, :], pS[0][:, :], ACT.Copy).then_inc(hhi_ready, 1)
                    split(B + n0 + 3, it)
                    act.wait_ge(slots_used, B + n0 + 2 + ITEM * it)
                    act.wait_ge(hmul_ready, done)
                    act.activation(sg[:, :], pG[:, :], ACT.Silu).then_inc(silu_ready, 1)
                    split(B + n0 + 4, it)
                    split(B + n0 + 5, it)
                    if c >= 1:
                        split(B + n0 + 6, it)
                        split(B + n0 + 7, it)
                    if c == 4:
                        act.wait_ge(pg_turned, it + 1)
                        act.activation(pgT, pS[1][:, 0:NT * P].rearrange("p (t s) -> p t s", t=NT),
                                       ACT.Copy).then_inc(pgT_ready, 1)
                act.wait_ge(h_turned, CHUNKS + CHUNKS * it)
                act.activation(hT_hi[:, :], pS[0][:, :], ACT.Copy).then_inc(hhi_ready, 1)
                split(B + ITEM, it)
                evacuate_gather(it + 1)
                split(B + ITEM + 1, it)
                act.wait_ge(slots_used, B + ITEM + ITEM * it)
                for c in range(2):
                    act.activation(y_sb[:, c * BANK:(c + 1) * BANK], pY[c][:, :], ACT.Copy).then_inc(y_copied, 1)

            for n in range(2):
                split(n)
            mix(0)
            dense()
            mix(1)
            route()
            with act.Fori(0, E) as it:
                item(it)
            act.wait_ge(steer_ready, 2)
            extra = act.value_load(steer[0:1, OVER + 1:OVER + 2], min_val=0, max_val=OVER)
            with act.Fori(0, OVER) as j:
                with act.If(extra > j):
                    item(j + E)
            act.wait_ge(res_added, RES_BASE + 4 * E + 4 * extra)
            for t in range(NT):
                act.activation(hn[:, t, :], h[:, t, :], ACT.Square,
                               accum_out=stat[:, 0, 8 + t:9 + t]).then_inc(sq_ready, 1)
            for t in range(NT):
                act.wait_ge(ms_ready, 8 + t + 1)
                act.activation(stat[:, 2, 8 + t:9 + t], stat[:, 1, 8 + t:9 + t], ACT.Sqrt).then_inc(root_ready, 1)

        @block.vector
        def _(dve):
            def split(n, it=0, per=ITEM):
                dve.wait_ge(hi_ready, n + 1 + per * it)
                dve.tensor_tensor(slot_lo(n), raw[:, n % RAW, :], slot_hi(n).bitcast(F32),
                                  ALU.subtract).then_inc(lo_ready, 1)

            def split_half(n):
                dve.wait_ge(hi_ready, n + 1)
                dve.tensor_tensor(slot_lo(n)[:, 0:KT * P], raw[:, n % RAW, 0:KT * P],
                                  slot_hi(n)[:, 0:KT * P].bitcast(F32), ALU.subtract).then_inc(lo_ready, 1)

            def norm(m, turned=True):
                for t in range(NT):
                    k = 2 * m + t
                    dve.wait_ge(sq_ready, k + 1)
                    dve.tensor_scalar(stat[:, 1, k:k + 1], stat[:, 0, k:k + 1], 1.0 / D, EPS,
                                      ALU.mult, ALU.add).then_inc(ms_ready, 1)
                for t in range(NT):
                    k = 2 * m + t
                    dve.wait_ge(root_ready, k + 1)
                    dve.reciprocal(stat[:, 3, k:k + 1], stat[:, 2, k:k + 1]).then_inc(inv_ready, 1)
                    dve.wait_ge(inv_ready, k + 1)
                    dve.wait_ge(g_loaded[m % 2], 16 * (m // 2 + 1))
                    dve.scalar_tensor_tensor(out=hn[:, t, :], in0=h[:, t, :], scalar=stat[:, 3, k:k + 1],
                                             in1=g_bc[:, m % 2, :], op0=ALU.mult, op1=ALU.mult).then_inc(hn_ready, 1)
                if not turned:
                    return
                for t in range(NT):
                    for q in range(2):
                        n = 4 * m + 2 * t + q
                        hi = xT_hi[:, 4 * q:4 * q + 4, t * P:(t + 1) * P].bitcast(F32)
                        dve.wait_ge(xhi_ready, n + 1)
                        dve.tensor_tensor(xT_lo[:, 4 * q:4 * q + 4, t * P:(t + 1) * P],
                                          pS[2 * t + q][:, :].rearrange("p (k s) -> p k s", k=4), hi,
                                          ALU.subtract).then_inc(xlo_ready, 1)

            def add_residual(products, wait, first):
                for t in range(NT):
                    for c in range(2):
                        wait(2 * t + c)
                        if first is not None:
                            dve.wait_ge(res_added, first)
                        dve.tensor_tensor(h[:, t, c * BANK:(c + 1) * BANK], products[2 * t + c][:, :],
                                          h[:, t, c * BANK:(c + 1) * BANK], ALU.add).then_inc(res_added, 1)

            def mix_lo_of(dst, src, hi, count):
                dve.wait_ge(mixhi_ready, count)
                dve.tensor_tensor(dst, src, hi.bitcast(F32), ALU.subtract).then_inc(mixlo_ready, 1)

            def mix(layer):
                b = MIX_BASE[layer]
                f = b + MIX_IN_TOKEN
                pieces = (3 + CT) * layer
                norm(2 * layer)
                for n in range(b + 2, b + MIX_SLOTS + 2):
                    if n == f + MIX_IN_FEAT - 1:
                        split_half(n)
                    else:
                        split(n)
                    if n == b + 6:
                        dve.wait_ge(row_loaded, 16 * DEPTH * (3 + TAPS))
                        for t in range(NT):
                            k = NT * layer + t
                            s = 5 * k
                            v = uv_t[:, t, W_B:2 * W_B]
                            dve.wait_ge(uv_ready, 4 * layer + 3 + t)
                            dve.bn_stats(bn[:, k, :], v).then_inc(ln_step, 1)
                            dve.wait_ge(ln_step, s + 1)
                            dve.bn_aggr(mv[:, k, :], bn[:, k, :]).then_inc(ln_step, 1)
                            dve.wait_ge(ln_step, s + 2)
                            dve.tensor_scalar(vst[:, 0, k:k + 1], mv[:, k, 1:2], EPS, None,
                                              ALU.add).then_inc(ln_step, 1)
                            dve.wait_ge(ln_root, k + 1)
                            dve.reciprocal(vst[:, 2, k:k + 1], vst[:, 1, k:k + 1]).then_inc(ln_step, 1)
                            dve.wait_ge(ln_step, s + 4)
                            dve.tensor_scalar(v, v, mv[:, k, 0:1], vst[:, 2, k:k + 1], ALU.subtract,
                                              ALU.mult).then_inc(ln_step, 1)
                            dve.wait_ge(ln_step, s + 5)
                            dve.tensor_tensor(v, v, vg_bc[:, layer, :], ALU.mult).then_inc(vn_ready, 1)
                            dve.wait_ge(vn_ready, 2 * k + 1)
                            dve.tensor_tensor(v, v, vb_bc[:, layer, :], ALU.add).then_inc(vn_ready, 1)
                    if n == f + 3:
                        for g in range(AT):
                            dve.wait_ge(dft1_done, AT * layer + g + 1)
                            dve.tensor_copy(dft1_g[:, g, :], pS[g][:, :]).then_inc(dft1_ready, 1)
                    if n == f + 4:
                        mix_lo_of(mixT_lo[:, 0:AT, :], pS[0][:, :].rearrange("p (k s) -> p k s", k=AT),
                                  mixT_hi[:, 0:AT, :], pieces + 1)
                    if n == f + 5:
                        for t in range(NT):
                            dve.wait_ge(z_done, NT * layer + t + 1)
                            for hd in range(HEADS_B):
                                cols = slice(hd * HEAD, (hd + 1) * HEAD)
                                last = dve.scalar_tensor_tensor(
                                    out=uv_t[:, t, cols], in0=pS[2 + t][:, cols], scalar=bs[:, layer, hd:hd + 1],
                                    in1=uv_t[:, t, cols], op0=ALU.add, op1=ALU.mult)
                            last.then_inc(g_ready, 1)
                    if n == f + 6:
                        mix_lo_of(mixT_lo[:, AT:AT + 2, :], pS[1][:, :].rearrange("p (k s) -> p k s", k=2),
                                  mixT_hi[:, AT:AT + 2, :], pieces + 2)
                        mix_lo_of(mixT_lo[:, AT + 2, :], pS[0][:, 0:SEQ], mixT_hi[:, AT + 2, :], pieces + 3)
                    if n == b + 11:
                        dve.wait_ge(feat_ready, MIX_IN_FEAT * (layer + 1))
                        dve.wait_ge(masks_ready, MASKS)
                        for ft in range(CT):
                            s = 4 * (CT * layer + ft)
                            m = pad[:, ft, 1:SEQ + 1]
                            acc = feat[:, CT + ft, :]
                            dve.tensor_tensor(m, acc, feat[:, 2 * CT + ft, :], ALU.mult).then_inc(conv_step, 1)
                            dve.wait_ge(conv_step, s + 1)
                            for tap in range(TAPS):
                                w = cw[:, layer, tap * CT + ft:tap * CT + ft + 1]
                                src = pad[:, ft, tap:tap + SEQ]
                                if tap == 0:
                                    dve.tensor_scalar(acc, src, w, None, ALU.mult).then_inc(conv_step, 1)
                                else:
                                    dve.scalar_tensor_tensor(out=acc, in0=src, scalar=w, in1=acc, op0=ALU.mult,
                                                             op1=ALU.add).then_inc(conv_step, 1)
                                dve.wait_ge(conv_step, s + 2 + tap)
                            dve.tensor_tensor(feat[:, ft, :], feat[:, ft, :], acc, ALU.mult).then_inc(y_ready, 1)
                        for ft in range(CT):
                            mix_lo_of(mixT_lo[:, AT + BT + ft, :], feat[:, ft, :], mixT_hi[:, AT + BT + ft, :],
                                      pieces + 4 + ft)
                add_residual(OUT_BANK, lambda q: dve.wait_ge(slots_used, b + MIX_SLOTS), 8 * layer or None)

            def dense_step(n0, s, rounds):
                it = dict(it=rounds, per=RAW)
                split(n0 + 2, **it)
                split(n0 + 3, **it)
                multiply(n0 + 2 + RAW * rounds, s + 2 * rounds)
                split(n0 + 4, **it)
                dense_lo(s + 2 * rounds)

            def multiply(used, s):
                dve.wait_ge(silu_ready, s + 1)
                dve.wait_ge(hlo_ready, s)
                dve.wait_ge(slots_used, used)
                dve.tensor_tensor(hmul[:, :], pU[:, :], sg[:, :], ALU.mult).then_inc(hmul_ready, 1)

            def dense_lo(s):
                dve.wait_ge(hhi_ready, s + 1)
                dve.tensor_tensor(hT_lo[:, :], hmul[:, :], hT_hi[:, :].bitcast(F32), ALU.subtract).then_inc(hlo_ready, 1)

            def dense():
                norm(1)
                b = DENSE_BASE
                split(b + 2)
                split(b + 3)
                multiply(b + 2, 0)
                dense_lo(0)
                with dve.Fori(0, DENSE_STEPS // 2) as r:
                    for u in range(2):
                        dense_step(b + 2 + 3 * u, 1 + u, r)
                split(b + DENSE_SLOTS + 1)
                add_residual(pS, lambda q: dve.wait_ge(slots_used, b + DENSE_SLOTS), 4)

            def route():
                norm(3)
                dve.wait_ge(rwhi_ready, 1)
                dve.tensor_tensor(rw_lo[:, :, :], rw[:, :, :], rw_hi[:, :, :].bitcast(F32),
                                  ALU.subtract).then_inc(rwlo_ready, 1)
                for t in range(NT):
                    dve.wait_ge(hnhi_ready, t + 1)
                    dve.tensor_tensor(hn_lo[:, t, :], hn[:, t, :], hn_hi[:, t, :].bitcast(F32),
                                      ALU.subtract).then_inc(hnlo_ready, 1)
                steps = [0]

                def step(ins):
                    steps[0] += 1
                    ins.then_inc(route_step, 1)
                    dve.wait_ge(route_step, steps[0])

                dve.wait_ge(logits_done, 1)
                step(dve.tensor_copy(lg[:, :, :], pY0[:, 0:NT * E].rearrange("p (t e) -> p t e", t=NT)))
                for t in range(NT):
                    step(dve.max(top[:, t, :], lg[:, t, :]))
                    step(dve.max_index(topi[:, t, :], top[:, t, :], lg[:, t, :]))
                dve.tensor_tensor(rt[:, 0, :], top[:, :, 1], top[:, :, 0], ALU.subtract).then_inc(diff_ready, 1)
                step(dve.tensor_copy(topf[:, :, :], topi[:, :, :]))
                for t in range(NT):
                    for k in range(TOP_K):
                        step(dve.tensor_scalar(oh[:, 2 * t + k, :], iota[:, 0:E], topf[:, t, k:k + 1], None,
                                               ALU.is_equal))
                    last = dve.tensor_tensor(sel[:, t, :], oh[:, 2 * t, :], oh[:, 2 * t + 1, :], ALU.add)
                    last.then_inc(sel_ready, 1)
                dve.wait_ge(exp_ready, 1)
                step(dve.tensor_scalar(rt[:, 3, :], rt[:, 1, :], 1.0, None, ALU.add))
                step(dve.reciprocal(rt[:, 2, :], rt[:, 3, :]))
                step(dve.tensor_tensor(rt[:, 3, :], rt[:, 1, :], rt[:, 2, :], ALU.mult))
                for t in range(NT):
                    step(dve.tensor_scalar(oh[:, 2 * t, :], oh[:, 2 * t, :], rt[:, 2, t:t + 1], None, ALU.mult))
                    step(dve.scalar_tensor_tensor(out=tab[:, 0:E, GATE + t], in0=oh[:, 2 * t + 1, :],
                                                  scalar=rt[:, 3, t:t + 1], in1=oh[:, 2 * t, :], op0=ALU.mult,
                                                  op1=ALU.add))
                    step(dve.tensor_copy(tab[:, 0:E, SEL + t], sel[:, t, :]))
                step(dve.tensor_copy(tab[:, 0:E, EID], iota[:, 0:E]))
                dve.wait_ge(ranks_done, 1)
                for t in range(NT):
                    step(dve.tensor_copy(tab[:, 0:E, RANK + t], pY1[:, t * E:(t + 1) * E]))
                for t in range(NT):
                    last = dve.tensor_scalar(pick[:, t, :], iota[:, :], tab[:, 0, RANK + t:RANK + t + 1],
                                             tab[:, 0, SEL + t:SEL + t + 1], ALU.is_equal, ALU.mult)
                last.then_inc(pick_ready, 1)
                evacuate_gather(0)
                step(dve.tensor_scalar(over[:, 0, :], pY1[:, NT * E:(NT + 1) * E], float(P), None, ALU.is_gt))
                step(dve.tensor_tensor_scan(over[:, 1, :], ones[:, 0:E], over[:, 0, :], 0.0, ALU.mult, ALU.add))
                for j in range(OVER):
                    step(dve.scalar_tensor_tensor(out=ohj[:, j, :], in0=over[:, 1, :], scalar=float(j + 1),
                                                  in1=over[:, 0, :], op0=ALU.is_equal, op1=ALU.mult))
                    step(dve.tensor_tensor(prod[:, :, :], tab[:, 0:E, :].rearrange("p e c -> p c e"),
                                           ohj[:, j:j + 1, :].to_broadcast([P, TAB, E]), ALU.mult))
                    step(dve.tensor_reduce(tab[:, E + j, :], prod[:, :, :], AX.X, ALU.add))
                step(dve.tensor_scalar(tab[:, E:E + OVER, RANK:RANK + NT], tab[:, E:E + OVER, RANK:RANK + NT],
                                       -float(P), None, ALU.add))
                dve.tensor_copy(steer[0:1, 0:OVER + 1], tab[0:1, E:E + OVER + 1, EID]).then_inc(steer_ready, 1)
                dve.tensor_copy(steer[0:1, OVER + 1:OVER + 2], over[0:1, 1, E - 1:E]).then_inc(steer_ready, 1)

            def evacuate_gather(g):
                for q, bank in enumerate((pS[3], pU)):
                    dve.wait_ge(gathered, 4 * g + q + 3)
                    dve.tensor_copy(xT_lo[:, 4 * q:4 * q + 4, 0:P],
                                    bank[:, :].rearrange("p (k s) -> p k s", k=4)).then_inc(gxlo_ready, 1)

            H0 = DENSE_STEPS

            def item(it):
                B = MOE_BASE

                def hT_low(c):
                    dve.wait_ge(hhi_ready, H0 + c + 1 + CHUNKS * it)
                    dve.tensor_tensor(hT_lo[:, :], pS[0][:, :], hT_hi[:, :].bitcast(F32),
                                      ALU.subtract).then_inc(hlo_ready, 1)

                for c in range(CHUNKS):
                    n0 = chunk_slot(c)
                    split(B + n0 + 2, it)
                    if c >= 1:
                        hT_low(c - 1)
                    for k in range(3, 6):
                        split(B + n0 + k, it)
                    if c >= 1:
                        dve.wait_ge(h_turned, c + CHUNKS * it)
                    multiply(B + n0 + 4 + ITEM * it, H0 + c + CHUNKS * it)
                    if c >= 1:
                        for k in range(6, 8):
                            split(B + n0 + k, it)
                    if c == 3:
                        dve.wait_ge(gathered, 4 * it + 4)
                        dve.tensor_copy(cur[:, :, :], tab[:, bass.ds(it, 2), :]).then_inc(cur_ready, 1)
                        dve.wait_ge(cur_ready, it + 1)
                        for t in range(NT):
                            last = dve.tensor_scalar(pick[:, t, :], iota[:, :], cur[:, 1, RANK + t:RANK + t + 1],
                                                     cur[:, 1, SEL + t:SEL + t + 1], ALU.is_equal, ALU.mult)
                        last.then_inc(pick_ready, 1)
                        for t in range(NT):
                            last = dve.tensor_scalar(pg[:, t, :], iota[:, :], cur[:, 0, RANK + t:RANK + t + 1],
                                                     cur[:, 0, GATE + t:GATE + t + 1], ALU.is_equal, ALU.mult)
                        last.then_inc(pg_ready, 1)
                hT_low(CHUNKS - 1)
                split(B + ITEM, it)
                evacuate_gather(it + 1)
                split(B + ITEM + 1, it)
                add_residual(pS, lambda q: dve.wait_ge(scattered, q + 1 + 4 * it), RES_BASE + 4 * it)

            for i in range(3):
                dve.wait_ge(ws_turned, i + 1)
                last = dve.tensor_copy(wsT[:, 4 * i:4 * i + 4, :],
                                       banks[i][:, :].rearrange("p (h q) -> p h q", h=4))
            last.then_inc(wsT_ready, 1)
            for n in range(2):
                split(n)
            mix(0)
            dense()
            mix(1)
            route()
            with dve.Fori(0, E) as it:
                item(it)
            dve.wait_ge(steer_ready, 2)
            extra = dve.value_load(steer[0:1, OVER + 1:OVER + 2], min_val=0, max_val=OVER)
            with dve.Fori(0, OVER) as j:
                with dve.If(extra > j):
                    item(j + E)
            norm(4, turned=False)

        @block.tensor
        def _(pe):
            def product(dst, a_hi, a_lo, b_hi, b_lo, first, last):
                pe.matmul(dst, a_hi, b_hi, start=first, stop=False)
                pe.matmul(dst, a_hi, b_lo, start=False, stop=False)
                return pe.matmul(dst, a_lo, b_hi, start=False, stop=last)

            def token_product(dst, t, k, w_of, n, first, last):
                return product(dst, xT_hi[:, k, t * P:(t + 1) * P], xT_lo[:, k, t * P:(t + 1) * P],
                               w_of(slot_hi(n)), w_of(slot_lo(n)), first, last)

            def feature_tile(dst, n, col, width=2 * P):
                for k in range(KT):
                    last = product(dst, eight_k(slot_hi(n), width)[:, k, col:col + P],
                                   eight_k(slot_lo(n), width)[:, k, col:col + P], xT_hi[:, k, :], xT_lo[:, k, :],
                                   k == 0, k == KT - 1)
                return last

            def turn_normed(m):
                for t in range(NT):
                    pe.wait_ge(hn_ready, 2 * m + t + 1)
                    for q in range(2):
                        for k in range(4):
                            last = pe.transpose(pS[2 * t + q][:, k * P:(k + 1) * P],
                                                hn[:, t, (4 * q + k) * P:(4 * q + k + 1) * P], ident[:, :])
                        last.then_inc(hn_turned, 1)

            def mix(layer):
                b = MIX_BASE[layer]
                f = b + MIX_IN_TOKEN
                pieces = (3 + CT) * layer
                turn_normed(2 * layer)
                pe.wait_ge(xlo_ready, 8 * layer + 4)
                for i in range(MIX_IN_TOKEN):
                    n, j, kh = b + i, i // 2, i % 2
                    pe.wait_ge(lo_ready, n + 1)
                    for t in range(NT):
                        for k in range(4):
                            last = token_product(pS[2 * j + t][:, :], t, 4 * kh + k, lambda s: four_k(s)[:, k, :], n,
                                                 kh == 0 and k == 0, kh == 1 and k == 3)
                    last.then_inc(slots_used, 1)
                for i in range(MIX_IN_FEAT):
                    n = f + i
                    tiles = min(2, FEAT_TILES - 2 * i)
                    pe.wait_ge(lo_ready, n + 1)
                    if i == 4:
                        pe.wait_ge(feat_ready, MIX_IN_FEAT * layer + 1)
                    for ft in range(tiles):
                        last = feature_tile(FEAT_BANK[i][:, ft * SEQ:(ft + 1) * SEQ], n, ft * P, tiles * P)
                    last.then_inc(slots_used, 1)
                    if i == 0:
                        pe.wait_ge(dft_loaded, 32)
                        pe.wait_ge(a_ready, 2 * layer + 2)
                        pe.wait_ge(uv_ready, 4 * layer + 2)
                        for g in range(AT):
                            for t in range(NT):
                                last = pe.matmul(pS[g][:, :], a_sb[:, t, g * P:(g + 1) * P], cs[:, t, :],
                                                 start=t == 0, stop=t == NT - 1)
                            last.then_inc(dft1_done, 1)
                    if i == 1:
                        pe.wait_ge(dft1_ready, AT * (layer + 1))
                        for g in range(AT):
                            for part in range(2):
                                last = pe.matmul(pS[0][:, g * SEQ:(g + 1) * SEQ], bd[:, part, :],
                                                 dft1_g[:, g, part * SEQ:(part + 1) * SEQ],
                                                 start=part == 0, stop=part == 1)
                        last.then_inc(dft2_done, 1)
                    if i == 2:
                        pe.wait_ge(uv_ready, 4 * layer + 4)
                        for t in range(NT):
                            pe.wait_ge(vn_ready, 2 * (NT * layer + t + 1))
                            for hd in range(HEADS_B):
                                last = pe.matmul(pS[2 + t][:, hd * HEAD:(hd + 1) * HEAD],
                                                 wsT[:, layer * HEADS_B + hd, :],
                                                 uv_t[:, t, W_B + hd * HEAD:W_B + (hd + 1) * HEAD],
                                                 start=True, stop=True)
                            last.then_inc(z_done, 1)
                    if i == 3:
                        pe.wait_ge(g_ready, NT * (layer + 1))
                        for k in range(BT):
                            if k == 2:
                                pe.wait_ge(mixlo_ready, pieces + 1)
                            for t in range(NT):
                                bank, col = (pS[1], k * SEQ) if k < 2 else (pS[0], 0)
                                last = pe.transpose(bank[:, col + t * P:col + (t + 1) * P],
                                                    uv_t[:, t, k * P:(k + 1) * P], ident[:, :])
                            if k >= 1:
                                last.then_inc(g_turned, 1)
                pe.wait_ge(feat_ready, MIX_IN_FEAT * layer + 3)
                for i in range(MIX_OUT):
                    n = b + MIX_IN + i
                    pe.wait_ge(lo_ready, n + 1)
                    pe.wait_ge(mixlo_ready, pieces + (1, 2, 4, 6)[i])
                    for kk in range(2):
                        k = 2 * i + kk
                        for t in range(NT):
                            rows = slice(t * P, (t + 1) * P)
                            for c in range(2):
                                cols = slice(c * BANK, (c + 1) * BANK)
                                last = product(OUT_BANK[2 * t + c][:, :], mixT_hi[:, k, rows], mixT_lo[:, k, rows],
                                               two_k(slot_hi(n))[:, kk, cols], two_k(slot_lo(n))[:, kk, cols],
                                               k == 0, k == KT - 1)
                    last.then_inc(slots_used, 1)

            def up_slot(n, dst, rounds):
                pe.wait_ge(lo_ready, n + 1 + RAW * rounds)
                for ft in range(2):
                    last = feature_tile(dst[:, ft * SEQ:(ft + 1) * SEQ], n, ft * P)
                last.then_inc(slots_used, 1)

            def down_slot(n, s, rounds, first=False, final=False):
                pe.wait_ge(lo_ready, n + 1 + RAW * rounds)
                pe.wait_ge(hlo_ready, s + 1 + 2 * rounds)
                for ft in range(2):
                    for t in range(NT):
                        rows = slice(ft * SEQ + t * P, ft * SEQ + (t + 1) * P)
                        for c in range(2):
                            cols = slice(c * BANK, (c + 1) * BANK)
                            last = product(pS[2 * t + c][:, :], hT_hi[:, rows], hT_lo[:, rows],
                                           two_k(slot_hi(n))[:, ft, cols], two_k(slot_lo(n))[:, ft, cols],
                                           first and ft == 0, final and ft == 1)
                last.then_inc(slots_used, 1)

            def dense_step(n0, s, rounds, first=False):
                pe.wait_ge(silu_ready, s + 2 * rounds)
                up_slot(n0, pG, rounds)
                pe.wait_ge(hmul_ready, s + 2 * rounds)
                up_slot(n0 + 1, pU, rounds)
                down_slot(n0 + 2, s - 1, rounds, first=first)

            def dense():
                b = DENSE_BASE
                turn_normed(1)
                pe.wait_ge(xlo_ready, 8)
                up_slot(b, pG, 0)
                up_slot(b + 1, pU, 0)
                for u in range(2):
                    dense_step(b + 2 + 3 * u, 1 + u, 0, first=u == 0)
                with pe.Fori(1, DENSE_STEPS // 2) as r:
                    for u in range(2):
                        dense_step(b + 2 + 3 * u, 1 + u, r)
                down_slot(b + DENSE_SLOTS - 1, DENSE_STEPS - 1, 0, final=True)

            def gather(count):
                pe.wait_ge(pick_ready, count)
                for part, dst in ((hn_hi, (pS[1], pS[2])), (hn_lo, (pS[3], pU))):
                    for q in range(2):
                        for k in range(4):
                            cols = slice((4 * q + k) * P, (4 * q + k + 1) * P)
                            for t in range(NT):
                                last = pe.matmul(dst[q][:, k * P:(k + 1) * P], part[:, t, cols], pick[:, t, :],
                                                 start=t == 0, stop=t == NT - 1)
                        last.then_inc(gathered, 1)

            def route():
                turn_normed(3)
                pe.wait_ge(xlo_ready, 16)
                pe.wait_ge(rwlo_ready, 1)
                for t in range(NT):
                    for k in range(KT):
                        x_hi, x_lo = xT_hi[:, k, t * P:(t + 1) * P], xT_lo[:, k, t * P:(t + 1) * P]
                        dst = pY0[:, t * E:(t + 1) * E]
                        pe.matmul(dst, x_lo, rw_lo[:, k, :], start=k == 0, stop=False)
                        last = product(dst, x_hi, x_lo, rw_hi[:, k, :], rw_lo[:, k, :], False, k == KT - 1)
                last.then_inc(logits_done, 1)
                pe.wait_ge(sel_ready, NT)
                pe.matmul(pY1[:, 0:E], before[:, :], sel[:, 0, :], start=True, stop=True)
                for dst, own in ((pY1[:, E:2 * E], before), (pY1[:, 2 * E:3 * E], ones)):
                    pe.matmul(dst, ones[:, :], sel[:, 0, :], start=True, stop=False)
                    last = pe.matmul(dst, own[:, :], sel[:, 1, :], start=False, stop=True)
                last.then_inc(ranks_done, 1)
                pe.wait_ge(hnlo_ready, NT)
                gather(1)

            H0 = DENSE_STEPS

            def item(it):
                B = MOE_BASE

                def up_half(i, k0, dst):
                    pe.wait_ge(lo_ready, B + i + 1 + ITEM * it)
                    for k in range(4):
                        last = token_product(dst[:, :], 0, k0 + k, lambda s: four_k(s)[:, k, :], B + i,
                                             k0 + k == 0, k0 + k == KT - 1)
                    last.then_inc(slots_used, 1)

                def turn_h(c):
                    pe.wait_ge(hmul_ready, H0 + c + 1 + CHUNKS * it)
                    if c == 0:
                        pe.wait_ge(res_added, RES_BASE + 4 * it)
                    else:
                        pe.wait_ge(hlo_ready, H0 + c + CHUNKS * it)
                    for k in range(4):
                        last = pe.transpose(pS[0][:, k * P:(k + 1) * P], hmul[:, k * P:(k + 1) * P], ident[:, :])
                    last.then_inc(h_turned, 1)

                def down(i, c):
                    pe.wait_ge(hlo_ready, H0 + c + 1 + CHUNKS * it)
                    for half in range(2):
                        n = B + i + half
                        pe.wait_ge(lo_ready, n + 1 + ITEM * it)
                        for kk in range(2):
                            k = 2 * half + kk
                            for d in range(2):
                                cols = slice(d * BANK, (d + 1) * BANK)
                                last = product(pY[d][:, :], hT_hi[:, k * P:(k + 1) * P], hT_lo[:, k * P:(k + 1) * P],
                                               two_k(slot_hi(n))[:, kk, cols], two_k(slot_lo(n))[:, kk, cols],
                                               c == 0 and k == 0, c == CHUNKS - 1 and k == 3)
                        last.then_inc(slots_used, 1)

                pe.wait_ge(gxhi_ready, 2 * it + 2)
                pe.wait_ge(gxlo_ready, 2 * it + 2)
                for c in range(CHUNKS):
                    n0 = chunk_slot(c)
                    pe.wait_ge(silu_ready, H0 + c + CHUNKS * it)
                    up_half(n0, 0, pG)
                    if c >= 1:
                        turn_h(c - 1)
                    if c == 4:
                        pe.wait_ge(pg_ready, it + 1)
                        for t in range(NT):
                            last = pe.transpose(pS[1][:, t * P:(t + 1) * P], pg[:, t, :], ident[:, :])
                        last.then_inc(pg_turned, 1)
                    up_half(n0 + 1, 4, pG)
                    pe.wait_ge(hmul_ready, H0 + c + CHUNKS * it)
                    up_half(n0 + 2, 0, pU)
                    up_half(n0 + 3, 4, pU)
                    if c >= 1:
                        down(n0 + 4, c - 1)
                turn_h(CHUNKS - 1)
                pe.wait_ge(pgT_ready, it + 1)
                gather(it + 2)
                down(chunk_slot(CHUNKS), CHUNKS - 1)
                pe.wait_ge(y_copied, 2 * it + 2)
                pe.wait_ge(gxhi_ready, 2 * it + 4)
                pe.wait_ge(gxlo_ready, 2 * it + 4)
                for t in range(NT):
                    for c in range(2):
                        pe.matmul(pS[2 * t + c][:, :], pgT[:, t, :], y_sb[:, c * BANK:(c + 1) * BANK],
                                  start=True, stop=True).then_inc(scattered, 1)

            pe.wait_ge(masks_ready, 1)
            pe.wait_ge(ws_loaded, 16)
            for i in range(3):
                for k in range(4):
                    last = pe.transpose(banks[i][:, k * P:(k + 1) * P], ws_raw[:, 4 * i + k, :], ident[:, :])
                last.then_inc(ws_turned, 1)
            mix(0)
            dense()
            mix(1)
            route()
            with pe.Fori(0, E) as it:
                item(it)
            pe.wait_ge(steer_ready, 2)
            extra = pe.value_load(steer[0:1, OVER + 1:OVER + 2], min_val=0, max_val=OVER)
            with pe.Fori(0, OVER) as j:
                with pe.If(extra > j):
                    item(j + E)


def dft_tables(seq, head, per_tile):
    s = np.arange(seq)
    angle = 2 * np.pi * (np.outer(s, s) % seq) / seq
    over_seq = np.concatenate([np.cos(angle), np.sin(angle)], axis=1).astype(np.float32)
    d = np.arange(head)
    angle = 2 * np.pi * (np.outer(d, d) % head) / head
    scale = 1.0 / np.sqrt(seq * head)
    over_head = np.stack([np.kron(np.eye(per_tile), np.cos(angle) * scale),
                          np.kron(np.eye(per_tile), -np.sin(angle) * scale)]).astype(np.float32)
    return over_seq, over_head


_INS = ['x', 'norm_mix_g', 'w_in', 'vnorm_g', 'vnorm_b', 'w_spatial', 'b_spatial', 'conv_w', 'w_out',
        'norm_ffn_g', 'dense_w_gate', 'dense_w_up', 'dense_w_down', 'router_w',
        'moe_w_gate', 'moe_w_up', 'moe_w_down', 'norm_final_g']


def kernel(**inputs):
    import numpy as _np
    import concourse.bacc as _bacc
    from concourse import mybir as _mybir
    from concourse.bass_utils import run_bass_kernel_spmd as _run

    nc = _bacc.Bacc("TRN2", target_bir_lowering=False, num_devices=1)
    arrays, args = {}, []
    data = {name: _np.ascontiguousarray(inputs[name]) for name in _INS}
    seq = data['x'].shape[1]
    w_a = data['w_in'].shape[2] - 2 * data['vnorm_g'].shape[1] - 3 * data['conv_w'].shape[2]
    head = w_a // GROUPS_A
    data['dft_seq'], data['dft_head'] = dft_tables(seq, head, P // head)
    for name, a in data.items():
        arrays[f"in_{name}_dram"] = a
        args.append(nc.dram_tensor(f"in_{name}_dram", a.shape, _mybir.dt.from_np(a.dtype), kind="ExternalInput").ap())
    shape = data['x'].shape
    args.append(nc.dram_tensor("out_0_dram", shape, _mybir.dt.float32, kind="ExternalOutput").ap())
    hybrid_encoder(nc, *args)
    r = _run(nc, [arrays], core_ids=[0])
    return r.results[0]["out_0_dram"]
```

```python
import numpy as np

import concourse.bass as bass
from concourse import mybir
from contextlib import ExitStack

F32 = mybir.dt.float32
F32R = mybir.dt.float32r
I32 = mybir.dt.int32
U32 = mybir.dt.uint32
ALU = mybir.AluOpType
ACT = mybir.ActivationFunctionType
AX = mybir.AxisListType

P = 128
BANK = 512
EPS = 1e-6
TOP_K = 2
GROUPS_A = 4


def hybrid_encoder(nc, x, norm_mix_g, w_in, vnorm_g, vnorm_b, w_spatial, b_spatial, conv_w, w_out,
                   norm_ffn_g, dense_w_gate, dense_w_up, dense_w_down, router_w,
                   moe_w_gate, moe_w_up, moe_w_down, norm_final_g, dft_seq, dft_head, out):
    _, SEQ, D = x.shape
    DEPTH, _, D_IN = w_in.shape
    W_B = vnorm_g.shape[1]
    HEADS_B = b_spatial.shape[2]
    HEAD = W_B // HEADS_B
    TAPS, W_C = conv_w.shape[1:]
    W_A = D_IN - 2 * W_B - 3 * W_C
    F_DENSE = dense_w_gate.shape[2]
    E = router_w.shape[2]
    F_EXP = moe_w_gate.shape[3]
    NT = SEQ // P
    KT = D // P
    TOKEN_COLS = W_A + 2 * W_B
    FEAT_TILES = 3 * W_C // P
    CT = W_C // P
    AT = W_A // P
    BT = W_B // P
    assert NT == 2 and KT == 8 and TOKEN_COLS == 2 * BANK and SEQ == 2 * P and E == 8

    SLOT = 2048
    RAW = 6
    SPLIT = 3
    MIX_IN_TOKEN = 4
    MIX_IN_FEAT = -(-FEAT_TILES // 2)
    MIX_IN = MIX_IN_TOKEN + MIX_IN_FEAT
    MIX_OUT = KT // 2
    MIX_SLOTS = MIX_IN + MIX_OUT
    DENSE_STEPS = F_DENSE // (2 * P)
    DENSE_SLOTS = 3 * DENSE_STEPS
    CHUNKS = F_EXP // BANK
    ITEM = 6 * CHUNKS
    EXTRA = 5
    DEEP = RAW + EXTRA
    ROUNDS = [DEEP, DEEP, DEEP - 1, DEEP - 1]
    assert sum(ROUNDS) == ITEM
    ROUND_START = [sum(ROUNDS[:r]) for r in range(len(ROUNDS))]
    PLACE = [(p, r) for r, size in enumerate(ROUNDS) for p in range(size)]
    MIX_BASE = [0, MIX_SLOTS + DENSE_SLOTS]
    DENSE_BASE = MIX_SLOTS
    MOE_BASE = 2 * MIX_SLOTS + DENSE_SLOTS
    assert ITEM % SPLIT == 0 and DENSE_STEPS % 2 == 1

    OVER = (TOP_K * SEQ) // (P + 1)
    ITEMS = E + OVER
    TAB = 8
    RANK, SEL, GATE, EID = 0, 2, 4, 6
    RES_BASE = 3 * 4

    ctx = ExitStack()
    with ctx:
        def sb(name, shape, dt=F32):
            return ctx.enter_context(nc.sbuf_tensor(name, shape, dt))

        def sem(name):
            return ctx.enter_context(nc.semaphore(name))

        raw = sb("raw", [P, RAW, SLOT])
        w_hi = sb("w_hi", [P, SPLIT, SLOT], F32R)
        w_lo = sb("w_lo", [P, SPLIT, SLOT], F32R)
        h = sb("h", [P, NT, D])
        hn = sb("hn", [P, NT, D])
        xT_hi = sb("xT_hi", [P, KT, SEQ], F32R)
        xT_lo = sb("xT_lo", [P, KT, SEQ], F32R)
        mix_hi = sb("mix_hi", [P, KT * SEQ], F32R)
        mix_lo = sb("mix_lo", [P, KT * SEQ], F32R)
        mixT_hi = mix_hi[:, :].rearrange("p (k s) -> p k s", k=KT)
        mixT_lo = mix_lo[:, :].rearrange("p (k s) -> p k s", k=KT)
        hn_hi = mix_hi[:, :].rearrange("p (t d) -> p t d", t=NT)
        hn_lo = mix_lo[:, :].rearrange("p (t d) -> p t d", t=NT)
        late = sb("late", [P, EXTRA, SLOT])

        def in_late(slot, start, *dims):
            size = int(np.prod(dims))
            flat = late[:, slot:, :].rearrange("p x n -> p (x n)")[:, start:start + size]
            return flat.rearrange("p (a b) -> p a b", a=dims[0])

        cs = in_late(0, 0, NT, 2 * SEQ)
        bd = in_late(0, NT * 2 * SEQ, 2, P)
        vg_bc = in_late(0, NT * 2 * SEQ + 2 * P, DEPTH, W_B)
        wsT = in_late(1, 0, DEPTH * HEADS_B, P)
        uv_t = in_late(2, 0, NT, 2 * W_B)
        feat = in_late(3, 0, FEAT_TILES, SEQ)
        ws_raw = in_late(3, 0, DEPTH * HEADS_B, P)
        pad = in_late(3, FEAT_TILES * SEQ, CT, SEQ + 2)
        vb_bc = in_late(3, FEAT_TILES * SEQ + CT * (SEQ + 2), DEPTH, W_B)
        rw = in_late(1, DEPTH * HEADS_B * P, KT, E)
        sg = sb("sg", [P, BANK])
        dft1_more = sb("dft1_more", [P, BANK])
        dft1 = [sg[:, :], dft1_more[:, :]]
        ident = sb("ident", [P, P])
        before = sb("before", [P, P])
        ones = sb("ones", [P, P])
        iota = sb("iota", [P, P])
        g_bc = sb("g_bc", [P, 2, D])
        bs = sb("bs", [P, DEPTH, HEADS_B])
        cw = sb("cw", [P, DEPTH, TAPS * CT])
        rw_hi = sb("rw_hi", [P, KT, E], F32R)
        rw_lo = sb("rw_lo", [P, KT, E], F32R)
        hmul = sb("hmul", [P, BANK])
        a_sb = hmul[:, :].rearrange("p (t c) -> p t c", t=NT)
        assert NT * W_A == BANK
        hT_hi = sb("hT_hi", [P, BANK], F32R)
        hT_lo = sb("hT_lo", [P, BANK], F32R)
        y_hi, y_lo = xT_hi[:, :, P:2 * P], xT_lo[:, :, P:2 * P]
        pick = sb("pick", [P, NT, P], F32R)
        pickT = sb("pickT", [P, NT, P], F32R)
        tab = sb("tab", [P, ITEMS + 2, TAB])
        cur = sb("cur", [P, 2, TAB])
        stat = sb("stat", [P, 4, 2 * (DEPTH * 2 + 1)])
        bn = sb("bn", [P, DEPTH * NT, 6])
        mv = sb("mv", [P, DEPTH * NT, 2])
        vst = sb("vst", [P, 3, DEPTH * NT])
        eps_c = sb("eps_c", [P, 1])
        topi = sb("topi", [P, NT, E], U32)
        rt = sb("rt", [P, 4, NT])
        sel = sb("sel", [P, NT, E])
        places = np.cumsum([0, NT * E, NT * E, NT * E, 2 * NT * E, 2 * E, OVER * E, OVER * TAB * E]).tolist()
        lg, top, topf, oh, over, ohj, prod = (g_bc[:, 1, a:b].rearrange("p (t e) -> p t e", e=E)
                                              for a, b in zip(places, places[1:]))
        lgT = g_bc[0:E, 1, D - SEQ:D]
        assert places[-1] <= D - SEQ
        steer = sb("steer", [1, OVER + 2], I32)

        banks = [ctx.enter_context(nc.psum_tensor(n, [P, BANK], F32))
                 for n in ("pG", "pU", "pY0", "pY1", "pS0", "pS1", "pS2", "pS3")]
        pG, pU, pY0, pY1, *pS = banks
        pY = [pY0, pY1]
        FEAT_BANK = [pG, pU, pY0, pY1, pG]
        OUT_BANK = [pS[2], pS[3], pU, pY0]

        slot_loaded = [sem(f"slot_loaded{i}") for i in range(RAW)]
        expert_loaded = [sem(f"expert_loaded{i}") for i in range(DEEP)]
        hi_ready, lo_ready, slots_used = sem("hi_ready"), sem("lo_ready"), sem("slots_used")
        x_loaded = [sem(f"x_loaded{t}") for t in range(NT)]
        column_loaded = sem("column_loaded")
        ws_loaded, dft_loaded, row_loaded, rw_loaded = (sem("ws_loaded"), sem("dft_loaded"),
                                                        sem("row_loaded"), sem("rw_loaded"))
        g0_loaded = sem("g0_loaded")
        g_loaded = [sem(f"g_loaded{i}") for i in range(2)]
        eps_set = sem("eps_set")
        masks_set, masks_ready = sem("masks_set"), sem("masks_ready")
        ws_turned, wsT_ready = sem("ws_turned"), sem("wsT_ready")
        sq_ready, root_ready, inv_ready, hn_ready = (sem("sq_ready"), sem("root_ready"),
                                                               sem("inv_ready"), sem("hn_ready"))
        hn_turned, xhi_ready, xlo_ready = sem("hn_turned"), sem("xhi_ready"), sem("xlo_ready")
        a_ready, uv_ready, feat_ready = sem("a_ready"), sem("uv_ready"), sem("feat_ready")
        dft1_done, dft1_ready, dft2_done = sem("dft1_done"), sem("dft1_ready"), sem("dft2_done")
        ln_step, ln_root, vn_ready = sem("ln_step"), sem("ln_root"), sem("vn_ready")
        z_done, g_ready, g_turned = sem("z_done"), sem("g_ready"), sem("g_turned")
        conv_step, y_ready = sem("conv_step"), sem("y_ready")
        mixhi_ready, mixlo_ready = sem("mixhi_ready"), sem("mixlo_ready")
        res_added, first_tile_done = sem("res_added"), sem("first_tile_done")
        silu_ready, hmul_ready, h_turned, hhi_ready, hlo_ready = (sem("silu_ready"), sem("hmul_ready"), sem("h_turned"),
                                                                  sem("hhi_ready"), sem("hlo_ready"))
        rwhi_ready, rwlo_ready, logits_done = sem("rwhi_ready"), sem("rwlo_ready"), sem("logits_done")
        lgT_ready, logits_turned = sem("lgT_ready"), sem("logits_turned")
        hnhi_ready, hnlo_ready = sem("hnhi_ready"), sem("hnlo_ready")
        route_step, diff_ready, exp_ready, sel_ready, ranks_done, table_ready, steer_ready = (
            sem("route_step"), sem("diff_ready"), sem("exp_ready"), sem("sel_ready"), sem("ranks_done"),
            sem("table_ready"), sem("steer_ready"))
        cur_ready, pick_ready, pick_turned, pickT_ready = (sem("cur_ready"), sem("pick_ready"), sem("pick_turned"),
                                                           sem("pickT_ready"))
        gathered, gxhi_ready, gxlo_ready = sem("gathered"), sem("gxhi_ready"), sem("gxlo_ready")
        y_half_done = sem("y_half_done")
        yhi_ready, ylo_ready, scattered, stored = sem("yhi_ready"), sem("ylo_ready"), sem("scattered"), sem("stored")

        block = ctx.enter_context(nc.Block())

        def four_k(s):
            return s.rearrange("p (k n) -> p k n", n=BANK)

        def eight_k(s, n=2 * P):
            return s[:, 0:KT * n].rearrange("p (k n) -> p k n", n=n)

        def two_k(s):
            return s.rearrange("p (k n) -> p k n", n=D)

        deep_ring = [raw[:, (MOE_BASE + p) % RAW, :] for p in range(RAW)] + [late[:, p, :] for p in range(EXTRA)]

        def slot_raw(n):
            if n < MOE_BASE:
                return raw[:, n % RAW, :]
            return deep_ring[PLACE[(n - MOE_BASE) % ITEM][0]]

        def wait_loaded(engine, n, it, per):
            if n < MOE_BASE:
                engine.wait_ge(slot_loaded[n % RAW], 16 * (n // RAW + 1) + 16 * (per // RAW) * it)
            else:
                items, i = divmod(n - MOE_BASE, ITEM)
                place, rnd = PLACE[i]
                in_item = sum(size > place for size in ROUNDS)
                engine.wait_ge(expert_loaded[place], 16 * (rnd + 1 + in_item * items) + 16 * in_item * it)

        def slot_hi(n):
            return w_hi[:, n % SPLIT, :]

        def slot_lo(n):
            return w_lo[:, n % SPLIT, :]

        K_LAST = [(0, 0), (0, 1), (1, 0), (1, 1)]
        TILE_LAST = [(0, 0), (1, 0), (0, 1), (1, 1)]

        def chunk_slot(c):
            return 6 * c - 2 if c else 0

        @block.sync
        def _(sp):
            for t in range(NT):
                sp.dma_start(h[:, t, :], x[0, t * P:(t + 1) * P, :]).then_inc(x_loaded[t], 16)
                if t == 0:
                    sp.dma_start(g_bc[:, 0, :], norm_mix_g[0:1, :].to_broadcast([P, D])).then_inc(g0_loaded, 16)

            def load(n, view, src, rounds=0):
                if n >= RAW:
                    sp.wait_ge(lo_ready, n - RAW + 1 + RAW * rounds)
                sp.dma_start(view(slot_raw(n)), src).then_inc(slot_loaded[n % RAW], 16)

            def small_loads(i):
                if i == 2:
                    sp.dma_start(ws_raw, w_spatial.rearrange("l h p q -> p (l h) q")).then_inc(ws_loaded, 16)
                if i == 3:
                    sp.dma_start(cs[:, :, :], dft_seq.rearrange("(t p) n -> p t n", p=P)).then_inc(dft_loaded, 16)
                    sp.dma_start(bd[:, :, :], dft_head.rearrange("c p n -> p c n")).then_inc(dft_loaded, 16)
                if i == MIX_IN_TOKEN:
                    for layer in range(DEPTH):
                        sp.dma_start(vg_bc[:, layer, :], vnorm_g[layer:layer + 1, :].to_broadcast([P, W_B])) \
                            .then_inc(row_loaded, 16)
                        sp.dma_start(vb_bc[:, layer, :], vnorm_b[layer:layer + 1, :].to_broadcast([P, W_B])) \
                            .then_inc(row_loaded, 16)

            def mix_loads(layer):
                b = MIX_BASE[layer]
                w = w_in[layer].rearrange("(k p) n -> p k n", p=P)
                for i in range(MIX_IN_TOKEN):
                    if layer == 0:
                        small_loads(i)
                    j, kh = i // 2, i % 2
                    load(b + i, four_k, w[:, 4 * kh:4 * kh + 4, j * BANK:(j + 1) * BANK])
                if layer == 0:
                    small_loads(MIX_IN_TOKEN)
                for i in range(MIX_IN_FEAT):
                    c0 = TOKEN_COLS + 2 * P * i
                    n = min(2 * P, D_IN - c0)
                    load(b + MIX_IN_TOKEN + i, lambda s: eight_k(s, n), w[:, :, c0:c0 + n])
                w = w_out[layer].rearrange("(k p) n -> p k n", p=P)
                for i in range(MIX_OUT):
                    load(b + MIX_IN + i, two_k, w[:, 2 * i:2 * i + 2, :])

            def dense_load(n, w, s, rounds=0):
                if w is dense_w_down:
                    view, src = two_k, w[0].rearrange("(f p) n -> p f n", p=P)[:, bass.ds(2 * s, 2), :]
                else:
                    view, src = eight_k, w[0].rearrange("(k p) n -> p k n", p=P)[:, :, bass.ds(2 * P * s, 2 * P)]
                load(n, view, src, rounds)

            mix_loads(0)
            dense_load(DENSE_BASE, dense_w_gate, 0)
            dense_load(DENSE_BASE + 1, dense_w_up, 0)
            with sp.Fori(0, DENSE_STEPS // 2) as r:
                for u in range(2):
                    n0 = DENSE_BASE + 2 + 3 * u
                    dense_load(n0, dense_w_gate, 2 * r + 1 + u, r)
                    dense_load(n0 + 1, dense_w_up, 2 * r + 1 + u, r)
                    dense_load(n0 + 2, dense_w_down, 2 * r + u, r)
            dense_load(DENSE_BASE + DENSE_SLOTS - 1, dense_w_down, DENSE_STEPS - 1)
            mix_loads(1)

            def experts_load(i, view, src, it):
                place, rnd = PLACE[i]
                if it is not None:
                    before_it = ROUND_START[rnd - 1] + place
                    if place == DEEP - 1 and rnd == 0:
                        before_it = ROUND_START[1] + place
                    if rnd == 0:
                        before_it -= ITEM
                    sp.wait_ge(lo_ready, MOE_BASE + before_it + 1 + ITEM * it)
                elif place < RAW:
                    sp.wait_ge(lo_ready, MOE_BASE + i - RAW + 1)
                else:
                    if place == RAW:
                        sp.wait_ge(dft2_done, DEPTH)
                        sp.wait_ge(vn_ready, 2 * NT * DEPTH)
                    if place == RAW + 1:
                        sp.wait_ge(z_done, NT * DEPTH)
                    if place == RAW + 2:
                        sp.wait_ge(g_turned, 2 * DEPTH)
                    if place == RAW + 3:
                        sp.wait_ge(mixlo_ready, (3 + CT) * DEPTH)
                sp.dma_start(view(slot_raw(MOE_BASE + i)), src).then_inc(expert_loaded[place], 16)

            def item_load(i, expert, it):
                def of(e):
                    return bass.ds(e, 1)

                c = 0 if i < 4 else (i + 2) // 6
                k = i - chunk_slot(c)
                if i >= chunk_slot(CHUNKS):
                    c, k = CHUNKS, i - chunk_slot(CHUNKS) + 4
                if k < 4:
                    w = moe_w_gate if k < 2 else moe_w_up
                    src = w[0, of(expert), (k % 2) * D // 2:(k % 2 + 1) * D // 2, c * BANK:(c + 1) * BANK]
                    experts_load(i, four_k, src.rearrange("o (k p) n -> p (o k) n", p=P), it)
                else:
                    f0 = (c - 1) * BANK + (k - 4) * 2 * P
                    src = moe_w_down[0, of(expert), f0:f0 + 2 * P, :]
                    experts_load(i, two_k, src.rearrange("o (f p) n -> p (o f) n", p=P), it)

            for i in range(DEEP):
                item_load(i, 0, None)
            with sp.Fori(0, E - 1) as it:
                for i in range(DEEP, ITEM):
                    item_load(i, it, it)
                for i in range(DEEP):
                    item_load(i, it + 1, it + 1)
            for i in range(DEEP, ITEM):
                item_load(i, E - 1, E - 1)
            sp.wait_ge(steer_ready, 2)
            extra = sp.value_load(steer[0:1, OVER + 1:OVER + 2], min_val=0, max_val=OVER)
            first = sp.value_load(steer[0:1, 0:1], min_val=0, max_val=E - 1)
            for i in range(2):
                item_load(i, first, E)
            with sp.Fori(0, OVER) as j:
                with sp.If(extra > j):
                    mine = sp.value_load(steer[0:1, bass.ds(j, 1)], min_val=0, max_val=E - 1)
                    for i in range(2, ITEM):
                        item_load(i, mine, j + E)
                    following = sp.value_load(steer[0:1, bass.ds(j + 1, 1)], min_val=0, max_val=E - 1)
                    for i in range(2):
                        item_load(i, following, j + E + 1)
            for t in range(NT):
                sp.wait_ge(hn_ready, 4 * 2 * DEPTH + 2 * t + 2)
                sp.dma_start(out[0, t * P:(t + 1) * P, :], hn[:, t, :]).then_inc(stored, 16)
            sp.wait_ge(stored, 16 * NT)

        @block.gpsimd
        def _(pool):
            gains = [None, norm_ffn_g[0:1, :], norm_mix_g[1:2, :], norm_ffn_g[1:2, :],
                     norm_final_g.rearrange("(o n) -> o n", o=1)]

            def load_gain(m):
                pool.dma_start(g_bc[:, m % 2, :], gains[m].to_broadcast([P, D])).then_inc(g_loaded[m % 2], 16)

            pool.memset(eps_c[:, :], EPS).then_inc(eps_set, 1)
            pool.memset(ident[:, :], 0.0).then_inc(masks_set, 1)
            pool.wait_ge(masks_set, 1)
            pool.affine_select(out=ident[:, :], in_=ident[:, :], compare_op=ALU.not_equal, fill=1.0, base=0,
                               pattern=[[-1, P]], channel_multiplier=1).then_inc(masks_ready, 1)
            pool.memset(ones[:, :], 1.0).then_inc(masks_set, 1)
            pool.wait_ge(masks_set, 2)
            pool.affine_select(out=before[:, :], in_=ones[:, :], compare_op=ALU.is_gt, fill=0.0, base=0,
                               pattern=[[1, P]], channel_multiplier=-1).then_inc(masks_ready, 1)
            pool.memset(pad[:, :, 0:1], 0.0).then_inc(masks_ready, 1)
            pool.memset(pad[:, :, SEQ + 1:SEQ + 2], 0.0).then_inc(masks_ready, 1)
            pool.iota(iota[:, :], pattern=[[1, P]], base=0, channel_multiplier=0,
                      allow_small_or_imprecise_dtypes=True).then_inc(masks_ready, 1)
            pool.memset(tab[:, :, :], 0.0).then_inc(masks_ready, 1)
            pool.wait_ge(slots_used, 1)
            for layer in range(DEPTH):
                pool.dma_start(bs[:, layer, :], b_spatial[layer]).then_inc(column_loaded, 16)
                for tap in range(TAPS):
                    pool.dma_start(cw[:, layer, tap * CT:(tap + 1) * CT],
                                   conv_w[layer, tap, :].rearrange("(f p) -> p f", p=P),
                                   allow_slow_non_contiguous=True).then_inc(column_loaded, 16)
            load_gain(1)
            pool.dma_start(rw[:, :, :], router_w[0].rearrange("(k p) e -> p k e", p=P)).then_inc(rw_loaded, 16)
            for m in range(2, len(gains)):
                pool.wait_ge(hn_ready, 4 * (m - 2) + 4)
                load_gain(m)

        MASKS = 6

        @block.scalar
        def _(act):
            def split(n, it=0, per=ITEM):
                wait_loaded(act, n, it, per)
                if n >= SPLIT:
                    act.wait_ge(slots_used, n - SPLIT + 1 + per * it)
                act.activation(slot_hi(n), slot_raw(n), ACT.Copy).then_inc(hi_ready, 1)

            def split_half(n):
                act.wait_ge(slot_loaded[n % RAW], 16 * (n // RAW + 1))
                act.wait_ge(slots_used, n - SPLIT + 1)
                act.activation(slot_hi(n)[:, 0:KT * P], raw[:, n % RAW, 0:KT * P], ACT.Copy).then_inc(hi_ready, 1)

            def roots(m, wait):
                for t in range(NT):
                    k = 2 * m + t
                    wait(t)
                    act.activation(hn[:, t, :], h[:, t, :], ACT.Square, accum_out=stat[:, 0, k:k + 1]).then_inc(sq_ready, 1)
                    act.wait_ge(sq_ready, k + 1)
                    act.activation(stat[:, 1, k:k + 1], stat[:, 0, k:k + 1], ACT.Sqrt, bias=eps_c[:, 0:1],
                                   scale=1.0 / D).then_inc(root_ready, 1)

            def norm(m):
                def wait(t):
                    if m == 0:
                        act.wait_ge(x_loaded[t], 16)
                    else:
                        act.wait_ge(res_added, 4 * (m - 1) + 2 * (t + 1))
                        act.wait_ge(hn_ready, 4 * m)
                if m == 0:
                    act.wait_ge(eps_set, 1)
                act.activation(stat[:, 3, 0:1], eps_c[:, 0:1], ACT.Sqrt)
                roots(m, wait)
                if m == 0:
                    split(0)
                for t in range(NT):
                    for q in range(2):
                        act.wait_ge(hn_turned, 4 * m + 2 * t + q + 1)
                        act.activation(xT_hi[:, 4 * q:4 * q + 4, t * P:(t + 1) * P],
                                       pS[2 * t + q][:, :].rearrange("p (k s) -> p k s", k=4),
                                       ACT.Copy).then_inc(xhi_ready, 1)

            def mix(layer):
                b = MIX_BASE[layer]
                f = b + MIX_IN_TOKEN
                norm(2 * layer)
                if layer == 0:
                    split(1)
                for n in range(b + 2, b + MIX_SLOTS + 2):
                    if n == f + MIX_IN_FEAT - 1:
                        split_half(n)
                    else:
                        split(n)
                    if n == b + 4:
                        act.wait_ge(slots_used, b + 2)
                        for t in range(NT):
                            act.activation(a_sb[:, t, :], pS[t][:, 0:W_A], ACT.Copy).then_inc(a_ready, 1)
                        for t in range(NT):
                            act.activation(uv_t[:, t, 0:BANK - W_A], pS[t][:, W_A:BANK],
                                           ACT.Gelu_apprx_tanh).then_inc(uv_ready, 1)
                    if n == b + 6:
                        act.wait_ge(slots_used, b + 4)
                        for t in range(NT):
                            act.activation(uv_t[:, t, BANK - W_A:2 * W_B], pS[2 + t][:, :],
                                           ACT.Gelu_apprx_tanh).then_inc(uv_ready, 1)
                        for t in range(NT):
                            act.wait_ge(ln_step, 5 * (NT * layer + t) + 3)
                            k = NT * layer + t
                            act.activation(vst[:, 1, k:k + 1], vst[:, 0, k:k + 1], ACT.Sqrt).then_inc(ln_root, 1)
                    i = n - f - SPLIT
                    if 0 <= i < MIX_IN_FEAT:
                        act.wait_ge(slots_used, f + i + 1)
                        w = min(2, FEAT_TILES - 2 * i)
                        act.activation(feat[:, 2 * i:2 * i + w, :],
                                       FEAT_BANK[i][:, 0:w * SEQ].rearrange("p (f s) -> p f s", f=w),
                                       ACT.Copy).then_inc(feat_ready, 1)
                    if n == f + 4:
                        act.wait_ge(dft2_done, layer + 1)
                        act.activation(mixT_hi[:, 0:AT, :], pS[0][:, :].rearrange("p (k s) -> p k s", k=AT),
                                       ACT.Copy).then_inc(mixhi_ready, 1)
                    if n == f + 6:
                        act.wait_ge(g_turned, 2 * layer + 1)
                        act.activation(mixT_hi[:, AT:AT + 2, :], pS[1][:, :].rearrange("p (k s) -> p k s", k=2),
                                       ACT.Copy).then_inc(mixhi_ready, 1)
                        act.wait_ge(g_turned, 2 * layer + 2)
                        act.activation(mixT_hi[:, AT + 2, :], pS[0][:, 0:SEQ], ACT.Copy).then_inc(mixhi_ready, 1)
                    if n == b + 11:
                        for ft in range(CT):
                            act.wait_ge(y_ready, CT * layer + ft + 1)
                            act.activation(mixT_hi[:, AT + BT + ft, :], feat[:, ft, :],
                                           ACT.Copy).then_inc(mixhi_ready, 1)

            def dense_step(n0, s, rounds=0):
                it = dict(it=rounds, per=RAW)
                split(n0 + 2, **it)
                act.wait_ge(slots_used, n0 + 1 + RAW * rounds)
                act.wait_ge(hmul_ready, s + 2 * rounds)
                act.activation(sg[:, :], pG[:, :], ACT.Silu).then_inc(silu_ready, 1)
                split(n0 + 3, **it)
                split(n0 + 4, **it)
                act.wait_ge(hmul_ready, s + 1 + 2 * rounds)
                act.wait_ge(slots_used, n0 + 3 + RAW * rounds)
                act.activation(hT_hi[:, :], hmul[:, :], ACT.Copy).then_inc(hhi_ready, 1)

            def dense():
                norm(1)
                b = DENSE_BASE
                split(b + 2)
                act.wait_ge(slots_used, b + 1)
                act.activation(sg[:, :], pG[:, :], ACT.Silu).then_inc(silu_ready, 1)
                split(b + 3)
                act.wait_ge(hmul_ready, 1)
                act.activation(hT_hi[:, :], hmul[:, :], ACT.Copy).then_inc(hhi_ready, 1)
                with act.Fori(0, DENSE_STEPS // 2) as r:
                    for u in range(2):
                        dense_step(b + 2 + 3 * u, 1 + u, r)
                split(b + DENSE_SLOTS + 1)

            def evacuate_gather(g):
                for q in range(2):
                    act.wait_ge(gathered, 4 * g + q + 1)
                    act.activation(xT_hi[:, 4 * q:4 * q + 4, 0:P],
                                   pS[1 + q][:, :].rearrange("p (k s) -> p k s", k=4),
                                   ACT.Copy).then_inc(gxhi_ready, 1)

            def route():
                norm(3)
                for t in range(NT):
                    act.activation(hn_hi[:, t, :], hn[:, t, :], ACT.Copy).then_inc(hnhi_ready, 1)
                act.activation(stat[:, 3, 0:1], eps_c[:, 0:1], ACT.Exp)
                act.wait_ge(diff_ready, 1)
                act.activation(rt[:, 1, :], rt[:, 0, :], ACT.Exp).then_inc(exp_ready, 1)
                evacuate_gather(0)

            H0 = DENSE_STEPS

            def item(it):
                B = MOE_BASE
                act.activation(stat[:, 3, 0:1], eps_c[:, 0:1], ACT.Silu)
                for c in range(CHUNKS):
                    n0 = chunk_slot(c)
                    done = H0 + c + CHUNKS * it
                    split(B + n0 + 2, it)
                    if c >= 1:
                        act.wait_ge(h_turned, c + CHUNKS * it)
                        act.wait_ge(slots_used, B + n0 + ITEM * it)
                        act.activation(hT_hi[:, :], pS[0][:, :], ACT.Copy).then_inc(hhi_ready, 1)
                    split(B + n0 + 3, it)
                    act.wait_ge(slots_used, B + n0 + 2 + ITEM * it)
                    act.wait_ge(hmul_ready, done)
                    act.activation(sg[:, :], pG[:, :], ACT.Silu).then_inc(silu_ready, 1)
                    split(B + n0 + 4, it)
                    split(B + n0 + 5, it)
                    if c >= 1:
                        split(B + n0 + 6, it)
                        split(B + n0 + 7, it)
                    if c == 2:
                        act.wait_ge(pick_turned, it + 1)
                        act.activation(pickT[:, :, :], pS[1][:, 0:NT * P].rearrange("p (t s) -> p t s", t=NT),
                                       ACT.Copy).then_inc(pickT_ready, 1)
                act.wait_ge(h_turned, CHUNKS + CHUNKS * it)
                act.activation(hT_hi[:, :], pS[0][:, :], ACT.Copy).then_inc(hhi_ready, 1)
                split(B + ITEM, it)
                evacuate_gather(it + 1)
                split(B + ITEM + 1, it)
                for c in range(2):
                    if c == 0:
                        act.wait_ge(y_half_done, it + 1)
                    else:
                        act.wait_ge(slots_used, B + ITEM + ITEM * it)
                    act.activation(y_hi[:, 4 * c:4 * c + 4, :], pY[c][:, :].rearrange("p (k s) -> p k s", k=4),
                                   ACT.Copy).then_inc(yhi_ready, 1)

            mix(0)
            dense()
            act.wait_ge(rw_loaded, 16)
            act.activation(rw_hi[:, :, :], rw[:, :, :], ACT.Copy).then_inc(rwhi_ready, 1)
            mix(1)
            route()
            with act.Fori(0, E) as it:
                item(it)
            act.wait_ge(steer_ready, 2)
            extra = act.value_load(steer[0:1, OVER + 1:OVER + 2], min_val=0, max_val=OVER)
            with act.Fori(0, OVER) as j:
                with act.If(extra > j):
                    item(j + E)
            act.activation(stat[:, 3, 0:1], eps_c[:, 0:1], ACT.Sqrt)
            act.wait_ge(res_added, RES_BASE + 4 * E + 4 * extra)
            roots(4, lambda t: None)

        @block.vector
        def _(dve):
            def split(n, it=0, per=ITEM):
                dve.wait_ge(hi_ready, n + 1 + per * it)
                dve.tensor_tensor(slot_lo(n), slot_raw(n), slot_hi(n).bitcast(F32),
                                  ALU.subtract).then_inc(lo_ready, 1)

            def split_half(n):
                dve.wait_ge(hi_ready, n + 1)
                dve.tensor_tensor(slot_lo(n)[:, 0:KT * P], raw[:, n % RAW, 0:KT * P],
                                  slot_hi(n)[:, 0:KT * P].bitcast(F32), ALU.subtract).then_inc(lo_ready, 1)

            def norm(m, turned=True):
                for t in range(NT):
                    k = 2 * m + t
                    dve.wait_ge(root_ready, k + 1)
                    dve.reciprocal(stat[:, 2, k:k + 1], stat[:, 1, k:k + 1]).then_inc(inv_ready, 1)
                    dve.wait_ge(inv_ready, k + 1)
                    if m == 0:
                        dve.wait_ge(g0_loaded, 16)
                    else:
                        dve.wait_ge(g_loaded[m % 2], 16 * ((m + 1) // 2))
                    for q in range(2):
                        cols = slice(q * BANK, (q + 1) * BANK)
                        dve.scalar_tensor_tensor(out=hn[:, t, cols], in0=h[:, t, cols], scalar=stat[:, 2, k:k + 1],
                                                 in1=g_bc[:, m % 2, cols], op0=ALU.mult,
                                                 op1=ALU.mult).then_inc(hn_ready, 1)
                if not turned:
                    return
                if m == 0:
                    split(0)
                for t in range(NT):
                    for q in range(2):
                        n = 4 * m + 2 * t + q
                        hi = xT_hi[:, 4 * q:4 * q + 4, t * P:(t + 1) * P].bitcast(F32)
                        dve.wait_ge(xhi_ready, n + 1)
                        dve.tensor_tensor(xT_lo[:, 4 * q:4 * q + 4, t * P:(t + 1) * P],
                                          pS[2 * t + q][:, :].rearrange("p (k s) -> p k s", k=4), hi,
                                          ALU.subtract).then_inc(xlo_ready, 1)

            def add_residual(products, wait, first):
                for t in range(NT):
                    for c in range(2):
                        wait(2 * t + c)
                        if first is not None:
                            dve.wait_ge(res_added, first)
                        dve.tensor_tensor(h[:, t, c * BANK:(c + 1) * BANK], products[2 * t + c][:, :],
                                          h[:, t, c * BANK:(c + 1) * BANK], ALU.add).then_inc(res_added, 1)

            def finished(q, m, used):
                if q < 2:
                    dve.wait_ge(first_tile_done, m + 1)
                else:
                    dve.wait_ge(slots_used, used)

            def mix_lo_of(dst, src, hi, count):
                dve.wait_ge(mixhi_ready, count)
                dve.tensor_tensor(dst, src, hi.bitcast(F32), ALU.subtract).then_inc(mixlo_ready, 1)

            def mix(layer):
                b = MIX_BASE[layer]
                f = b + MIX_IN_TOKEN
                pieces = (3 + CT) * layer
                norm(2 * layer)
                if layer == 0:
                    split(1)
                for n in range(b + 2, b + MIX_SLOTS + 2):
                    if n == f + MIX_IN_FEAT - 1:
                        split_half(n)
                    else:
                        split(n)
                    if layer == 0 and n == b + 4:
                        for i in range(3):
                            dve.wait_ge(ws_turned, i + 1)
                            last = dve.tensor_copy(wsT[:, 4 * i:4 * i + 4, :],
                                                   banks[i][:, :].rearrange("p (h q) -> p h q", h=4))
                        last.then_inc(wsT_ready, 1)
                    if n == b + 6:
                        dve.wait_ge(row_loaded, 16 * DEPTH * 2)
                        dve.wait_ge(column_loaded, 16 * DEPTH * (1 + TAPS))
                        for t in range(NT):
                            k = NT * layer + t
                            s = 5 * k
                            v = uv_t[:, t, W_B:2 * W_B]
                            dve.wait_ge(uv_ready, 4 * layer + 3 + t)
                            dve.bn_stats(bn[:, k, :], v).then_inc(ln_step, 1)
                            dve.wait_ge(ln_step, s + 1)
                            dve.bn_aggr(mv[:, k, :], bn[:, k, :]).then_inc(ln_step, 1)
                            dve.wait_ge(ln_step, s + 2)
                            dve.tensor_scalar(vst[:, 0, k:k + 1], mv[:, k, 1:2], EPS, None,
                                              ALU.add).then_inc(ln_step, 1)
                            dve.wait_ge(ln_root, k + 1)
                            dve.reciprocal(vst[:, 2, k:k + 1], vst[:, 1, k:k + 1]).then_inc(ln_step, 1)
                            dve.wait_ge(ln_step, s + 4)
                            dve.tensor_scalar(v, v, mv[:, k, 0:1], vst[:, 2, k:k + 1], ALU.subtract,
                                              ALU.mult).then_inc(ln_step, 1)
                            dve.wait_ge(ln_step, s + 5)
                            dve.tensor_tensor(v, v, vg_bc[:, layer, :], ALU.mult).then_inc(vn_ready, 1)
                            dve.wait_ge(vn_ready, 2 * k + 1)
                            dve.tensor_tensor(v, v, vb_bc[:, layer, :], ALU.add).then_inc(vn_ready, 1)
                    if n == f + 3:
                        for g in range(AT):
                            dve.wait_ge(dft1_done, AT * layer + g + 1)
                            dve.tensor_copy(dft1[g], pS[g][:, :]).then_inc(dft1_ready, 1)
                    if n == f + 4:
                        mix_lo_of(mixT_lo[:, 0:AT, :], pS[0][:, :].rearrange("p (k s) -> p k s", k=AT),
                                  mixT_hi[:, 0:AT, :], pieces + 1)
                    if n == f + 5:
                        for t in range(NT):
                            dve.wait_ge(z_done, NT * layer + t + 1)
                            for hd in range(HEADS_B):
                                cols = slice(hd * HEAD, (hd + 1) * HEAD)
                                last = dve.scalar_tensor_tensor(
                                    out=uv_t[:, t, cols], in0=pS[2 + t][:, cols], scalar=bs[:, layer, hd:hd + 1],
                                    in1=uv_t[:, t, cols], op0=ALU.add, op1=ALU.mult)
                            last.then_inc(g_ready, 1)
                    if n == f + 6:
                        mix_lo_of(mixT_lo[:, AT:AT + 2, :], pS[1][:, :].rearrange("p (k s) -> p k s", k=2),
                                  mixT_hi[:, AT:AT + 2, :], pieces + 2)
                        mix_lo_of(mixT_lo[:, AT + 2, :], pS[0][:, 0:SEQ], mixT_hi[:, AT + 2, :], pieces + 3)
                    if n == b + 11:
                        dve.wait_ge(feat_ready, MIX_IN_FEAT * (layer + 1))
                        dve.wait_ge(masks_ready, MASKS)
                        for ft in range(CT):
                            s = 4 * (CT * layer + ft)
                            m = pad[:, ft, 1:SEQ + 1]
                            acc = feat[:, CT + ft, :]
                            dve.tensor_tensor(m, acc, feat[:, 2 * CT + ft, :], ALU.mult).then_inc(conv_step, 1)
                            dve.wait_ge(conv_step, s + 1)
                            for tap in range(TAPS):
                                w = cw[:, layer, tap * CT + ft:tap * CT + ft + 1]
                                src = pad[:, ft, tap:tap + SEQ]
                                if tap == 0:
                                    dve.tensor_scalar(acc, src, w, None, ALU.mult).then_inc(conv_step, 1)
                                else:
                                    dve.scalar_tensor_tensor(out=acc, in0=src, scalar=w, in1=acc, op0=ALU.mult,
                                                             op1=ALU.add).then_inc(conv_step, 1)
                                dve.wait_ge(conv_step, s + 2 + tap)
                            dve.tensor_tensor(feat[:, ft, :], feat[:, ft, :], acc, ALU.mult).then_inc(y_ready, 1)
                        for ft in range(CT):
                            mix_lo_of(mixT_lo[:, AT + BT + ft, :], feat[:, ft, :], mixT_hi[:, AT + BT + ft, :],
                                      pieces + 4 + ft)
                add_residual(OUT_BANK, lambda q: finished(q, 2 * layer, b + MIX_SLOTS), 8 * layer or None)

            def dense_step(n0, s, rounds):
                it = dict(it=rounds, per=RAW)
                split(n0 + 2, **it)
                split(n0 + 3, **it)
                multiply(n0 + 2 + RAW * rounds, s + 2 * rounds)
                split(n0 + 4, **it)
                dense_lo(s + 2 * rounds)

            def multiply(used, s):
                dve.wait_ge(silu_ready, s + 1)
                dve.wait_ge(hlo_ready, s)
                dve.wait_ge(slots_used, used)
                dve.tensor_tensor(hmul[:, :], pU[:, :], sg[:, :], ALU.mult).then_inc(hmul_ready, 1)

            def dense_lo(s):
                dve.wait_ge(hhi_ready, s + 1)
                dve.tensor_tensor(hT_lo[:, :], hmul[:, :], hT_hi[:, :].bitcast(F32), ALU.subtract).then_inc(hlo_ready, 1)

            def dense():
                norm(1)
                b = DENSE_BASE
                split(b + 2)
                split(b + 3)
                multiply(b + 2, 0)
                dense_lo(0)
                with dve.Fori(0, DENSE_STEPS // 2) as r:
                    for u in range(2):
                        dense_step(b + 2 + 3 * u, 1 + u, r)
                split(b + DENSE_SLOTS + 1)
                add_residual(pS, lambda q: finished(q, 1, b + DENSE_SLOTS), 4)

            def route():
                norm(3)
                for t in range(NT):
                    dve.wait_ge(hnhi_ready, t + 1)
                    dve.tensor_tensor(hn_lo[:, t, :], hn[:, t, :], hn_hi[:, t, :].bitcast(F32),
                                      ALU.subtract).then_inc(hnlo_ready, 1)
                steps = [0]

                def step(*results):
                    for ins in results:
                        steps[0] += 1
                        ins.then_inc(route_step, 1)
                    dve.wait_ge(route_step, steps[0])

                dve.wait_ge(logits_done, 1)
                dve.tensor_copy(lgT, pY0[0:E, 0:SEQ]).then_inc(lgT_ready, 1)
                dve.wait_ge(logits_turned, 1)
                step(dve.tensor_copy(lg, pY1[:, 0:NT * E].rearrange("p (t e) -> p t e", t=NT)))
                step(*[dve.max(top[:, t, :], lg[:, t, :]) for t in range(NT)])
                step(*[dve.max_index(topi[:, t, :], top[:, t, :], lg[:, t, :]) for t in range(NT)])
                dve.tensor_tensor(rt[:, 0, :], top[:, :, 1], top[:, :, 0], ALU.subtract).then_inc(diff_ready, 1)
                step(dve.tensor_copy(topf, topi[:, :, :]))
                step(*[dve.tensor_scalar(oh[:, 2 * t + k, :], iota[:, 0:E], topf[:, t, k:k + 1], None, ALU.is_equal)
                       for t in range(NT) for k in range(TOP_K)])
                oh_t = oh.rearrange("p (t k) e -> p t k e", t=NT)
                dve.tensor_tensor(sel[:, :, :], oh_t[:, :, 0, :], oh_t[:, :, 1, :], ALU.add).then_inc(sel_ready, 1)
                dve.wait_ge(sel_ready, 1)
                step(dve.tensor_copy(tab[:, 0:E, SEL:SEL + NT].rearrange("p e t -> p t e"), sel[:, :, :]))
                dve.wait_ge(exp_ready, 1)
                step(dve.tensor_scalar(rt[:, 3, :], rt[:, 1, :], 1.0, None, ALU.add))
                step(dve.reciprocal(rt[:, 2, :], rt[:, 3, :]))
                step(dve.tensor_tensor(rt[:, 3, :], rt[:, 1, :], rt[:, 2, :], ALU.mult))
                dve.wait_ge(ranks_done, 1)
                step(*[dve.tensor_copy(tab[:, 0:E, RANK + t], ranks[:, 0:E]) for t, ranks in enumerate((pG, pS[0]))])
                for t in range(NT):
                    last = dve.tensor_scalar(pick[:, t, :], iota[:, :], tab[:, 0, RANK + t:RANK + t + 1],
                                             tab[:, 0, SEL + t:SEL + t + 1], ALU.is_equal, ALU.mult)
                last.then_inc(pick_ready, 1)
                step(*[dve.tensor_scalar(oh[:, 2 * t, :], oh[:, 2 * t, :], rt[:, 2, t:t + 1], None, ALU.mult)
                       for t in range(NT)])
                step(*[dve.scalar_tensor_tensor(out=tab[:, 0:E, GATE + t], in0=oh[:, 2 * t + 1, :],
                                                scalar=rt[:, 3, t:t + 1], in1=oh[:, 2 * t, :], op0=ALU.mult,
                                                op1=ALU.add) for t in range(NT)],
                     dve.tensor_copy(tab[:, 0:E, EID], iota[:, 0:E]))
                dve.wait_ge(ranks_done, 2)
                step(dve.tensor_scalar(over[:, 0, :], pY0[:, 0:E], float(P), None, ALU.is_gt))
                step(dve.tensor_tensor_scan(over[:, 1, :], ones[:, 0:E], over[:, 0, :], 0.0, ALU.mult, ALU.add))
                step(*[dve.scalar_tensor_tensor(out=ohj[:, j, :], in0=over[:, 1, :], scalar=float(j + 1),
                                                in1=over[:, 0, :], op0=ALU.is_equal, op1=ALU.mult)
                       for j in range(OVER)])
                step(*[dve.tensor_tensor(prod[:, j * TAB:(j + 1) * TAB, :],
                                         tab[:, 0:E, :].rearrange("p e c -> p c e"),
                                         ohj[:, j:j + 1, :].to_broadcast([P, TAB, E]), ALU.mult)
                       for j in range(OVER)])
                step(dve.tensor_reduce(tab[:, E:E + OVER, :].rearrange("p e c -> p (e c)"), prod, AX.X, ALU.add))
                step(dve.tensor_scalar(tab[:, E:E + OVER, RANK:RANK + NT], tab[:, E:E + OVER, RANK:RANK + NT],
                                       -float(P), None, ALU.add))
                dve.tensor_copy(steer[0:1, 0:OVER + 1], tab[0:1, E:E + OVER + 1, EID]).then_inc(steer_ready, 1)
                dve.tensor_copy(steer[0:1, OVER + 1:OVER + 2], over[0:1, 1, E - 1:E]).then_inc(steer_ready, 1)
                evacuate_gather(0)

            def evacuate_gather(g):
                for q, bank in enumerate((pS[3], pU)):
                    dve.wait_ge(gathered, 4 * g + q + 3)
                    dve.tensor_copy(xT_lo[:, 4 * q:4 * q + 4, 0:P],
                                    bank[:, :].rearrange("p (k s) -> p k s", k=4)).then_inc(gxlo_ready, 1)

            H0 = DENSE_STEPS

            def item(it):
                B = MOE_BASE

                def hT_low(c):
                    dve.wait_ge(hhi_ready, H0 + c + 1 + CHUNKS * it)
                    dve.tensor_tensor(hT_lo[:, :], pS[0][:, :], hT_hi[:, :].bitcast(F32),
                                      ALU.subtract).then_inc(hlo_ready, 1)

                for c in range(CHUNKS):
                    n0 = chunk_slot(c)
                    split(B + n0 + 2, it)
                    if c >= 1:
                        hT_low(c - 1)
                    for k in range(3, 6):
                        split(B + n0 + k, it)
                    if c >= 1:
                        dve.wait_ge(h_turned, c + CHUNKS * it)
                    multiply(B + n0 + 4 + ITEM * it, H0 + c + CHUNKS * it)
                    if c >= 1:
                        for k in range(6, 8):
                            split(B + n0 + k, it)
                    if c == 3:
                        dve.wait_ge(pick_turned, it + 1)
                        dve.tensor_copy(cur[:, :, :], tab[:, bass.ds(it, 2), :]).then_inc(cur_ready, 1)
                        dve.wait_ge(cur_ready, it + 1)
                        for t in range(NT):
                            last = dve.tensor_scalar(pick[:, t, :], iota[:, :], cur[:, 1, RANK + t:RANK + t + 1],
                                                     cur[:, 1, SEL + t:SEL + t + 1], ALU.is_equal, ALU.mult)
                        last.then_inc(pick_ready, 1)
                hT_low(CHUNKS - 1)
                split(B + ITEM, it)
                evacuate_gather(it + 1)
                for c in range(2):
                    dve.wait_ge(yhi_ready, c + 1 + 2 * it)
                    dve.tensor_tensor(y_lo[:, 4 * c:4 * c + 4, :], pY[c][:, :].rearrange("p (k s) -> p k s", k=4),
                                      y_hi[:, 4 * c:4 * c + 4, :].bitcast(F32), ALU.subtract).then_inc(ylo_ready, 1)
                split(B + ITEM + 1, it)
                dve.wait_ge(res_added, RES_BASE + 4 * it)
                for c in range(2):
                    for t in range(NT):
                        cols = slice(c * BANK, (c + 1) * BANK)
                        dve.wait_ge(scattered, NT * c + t + 1 + 4 * it)
                        dve.scalar_tensor_tensor(out=h[:, t, cols], in0=pS[2 * t + c][:, :],
                                                 scalar=cur[:, 0, GATE + t:GATE + t + 1], in1=h[:, t, cols],
                                                 op0=ALU.mult, op1=ALU.add).then_inc(res_added, 1)

            mix(0)
            dense()
            dve.wait_ge(rwhi_ready, 1)
            dve.tensor_tensor(rw_lo[:, :, :], rw[:, :, :], rw_hi[:, :, :].bitcast(F32), ALU.subtract).then_inc(rwlo_ready, 1)
            mix(1)
            route()
            with dve.Fori(0, E) as it:
                item(it)
            dve.wait_ge(steer_ready, 2)
            extra = dve.value_load(steer[0:1, OVER + 1:OVER + 2], min_val=0, max_val=OVER)
            with dve.Fori(0, OVER) as j:
                with dve.If(extra > j):
                    item(j + E)
            norm(4, turned=False)

        @block.tensor
        def _(pe):
            def product(dst, a_hi, a_lo, b_hi, b_lo, first, last):
                pe.matmul(dst, a_hi, b_hi, start=first, stop=False)
                pe.matmul(dst, a_hi, b_lo, start=False, stop=False)
                return pe.matmul(dst, a_lo, b_hi, start=False, stop=last)

            def token_product(dst, t, k, w_of, n, first, last):
                return product(dst, xT_hi[:, k, t * P:(t + 1) * P], xT_lo[:, k, t * P:(t + 1) * P],
                               w_of(slot_hi(n)), w_of(slot_lo(n)), first, last)

            def feature_tile(dst, n, col, width=2 * P):
                for k in range(KT):
                    last = product(dst, eight_k(slot_hi(n), width)[:, k, col:col + P],
                                   eight_k(slot_lo(n), width)[:, k, col:col + P], xT_hi[:, k, :], xT_lo[:, k, :],
                                   k == 0, k == KT - 1)
                return last

            def keep_clock(bank, count):
                for _ in range(count):
                    pe.matmul(bank[:, 0:P], ident[:, :], ident[:, :], start=True, stop=True)

            def turn_normed(m):
                for t in range(NT):
                    for q in range(2):
                        pe.wait_ge(hn_ready, 4 * m + 2 * t + q + 1)
                        for k in range(4):
                            last = pe.transpose(pS[2 * t + q][:, k * P:(k + 1) * P],
                                                hn[:, t, (4 * q + k) * P:(4 * q + k + 1) * P], ident[:, :])
                        last.then_inc(hn_turned, 1)

            def mix(layer):
                b = MIX_BASE[layer]
                f = b + MIX_IN_TOKEN
                pieces = (3 + CT) * layer
                turn_normed(2 * layer)
                for i in range(MIX_IN_TOKEN):
                    n, j, kh = b + i, i // 2, i % 2
                    pe.wait_ge(lo_ready, n + 1)
                    for t in range(NT):
                        pe.wait_ge(xlo_ready, 8 * layer + 2 * t + kh + 1)
                        for k in range(4):
                            last = token_product(pS[2 * j + t][:, :], t, 4 * kh + k, lambda s: four_k(s)[:, k, :], n,
                                                 kh == 0 and k == 0, kh == 1 and k == 3)
                    last.then_inc(slots_used, 1)
                    if layer == 0 and i == 2:
                        pe.wait_ge(ws_loaded, 16)
                        for q in range(3):
                            for k in range(4):
                                last = pe.transpose(banks[q][:, k * P:(k + 1) * P], ws_raw[:, 4 * q + k, :],
                                                    ident[:, :])
                            last.then_inc(ws_turned, 1)
                for i in range(MIX_IN_FEAT):
                    n = f + i
                    tiles = min(2, FEAT_TILES - 2 * i)
                    pe.wait_ge(lo_ready, n + 1)
                    if i == 0:
                        pe.wait_ge(wsT_ready, 1)
                    if i == 4:
                        pe.wait_ge(feat_ready, MIX_IN_FEAT * layer + 1)
                    for ft in range(tiles):
                        last = feature_tile(FEAT_BANK[i][:, ft * SEQ:(ft + 1) * SEQ], n, ft * P, tiles * P)
                    last.then_inc(slots_used, 1)
                    if i == 0:
                        pe.wait_ge(dft_loaded, 32)
                        pe.wait_ge(a_ready, 2 * layer + 2)
                        pe.wait_ge(uv_ready, 4 * layer + 2)
                        for g in range(AT):
                            for t in range(NT):
                                last = pe.matmul(pS[g][:, :], a_sb[:, t, g * P:(g + 1) * P], cs[:, t, :],
                                                 start=t == 0, stop=t == NT - 1)
                            last.then_inc(dft1_done, 1)
                    if i == 1:
                        pe.wait_ge(dft1_ready, AT * (layer + 1))
                        for g in range(AT):
                            for part in range(2):
                                last = pe.matmul(pS[0][:, g * SEQ:(g + 1) * SEQ], bd[:, part, :],
                                                 dft1[g][:, part * SEQ:(part + 1) * SEQ],
                                                 start=part == 0, stop=part == 1)
                        last.then_inc(dft2_done, 1)
                    if i == 2:
                        pe.wait_ge(uv_ready, 4 * layer + 4)
                        for t in range(NT):
                            pe.wait_ge(vn_ready, 2 * (NT * layer + t + 1))
                            for hd in range(HEADS_B):
                                last = pe.matmul(pS[2 + t][:, hd * HEAD:(hd + 1) * HEAD],
                                                 wsT[:, layer * HEADS_B + hd, :],
                                                 uv_t[:, t, W_B + hd * HEAD:W_B + (hd + 1) * HEAD],
                                                 start=True, stop=True)
                            last.then_inc(z_done, 1)
                    if i == 3:
                        pe.wait_ge(g_ready, NT * (layer + 1))
                        for k in range(BT):
                            if k == 2:
                                pe.wait_ge(mixlo_ready, pieces + 1)
                            for t in range(NT):
                                bank, col = (pS[1], k * SEQ) if k < 2 else (pS[0], 0)
                                last = pe.transpose(bank[:, col + t * P:col + (t + 1) * P],
                                                    uv_t[:, t, k * P:(k + 1) * P], ident[:, :])
                            if k >= 1:
                                last.then_inc(g_turned, 1)
                pe.wait_ge(feat_ready, MIX_IN_FEAT * layer + 3)
                for i in range(MIX_OUT):
                    n = b + MIX_IN + i
                    pe.wait_ge(lo_ready, n + 1)
                    pe.wait_ge(mixlo_ready, pieces + (1, 2, 4, 6)[i])
                    for kk, t in TILE_LAST if i == MIX_OUT - 1 else K_LAST:
                        k = 2 * i + kk
                        rows = slice(t * P, (t + 1) * P)
                        for c in range(2):
                            cols = slice(c * BANK, (c + 1) * BANK)
                            last = product(OUT_BANK[2 * t + c][:, :], mixT_hi[:, k, rows], mixT_lo[:, k, rows],
                                           two_k(slot_hi(n))[:, kk, cols], two_k(slot_lo(n))[:, kk, cols],
                                           k == 0, k == KT - 1)
                        if i == MIX_OUT - 1 and kk == 1 and t == 0:
                            last.then_inc(first_tile_done, 1)
                    last.then_inc(slots_used, 1)

            def up_slot(n, dst, rounds):
                pe.wait_ge(lo_ready, n + 1 + RAW * rounds)
                for ft in range(2):
                    last = feature_tile(dst[:, ft * SEQ:(ft + 1) * SEQ], n, ft * P)
                last.then_inc(slots_used, 1)

            def down_slot(n, s, rounds, first=False, final=False):
                pe.wait_ge(lo_ready, n + 1 + RAW * rounds)
                pe.wait_ge(hlo_ready, s + 1 + 2 * rounds)
                for ft, t in TILE_LAST if final else K_LAST:
                    rows = slice(ft * SEQ + t * P, ft * SEQ + (t + 1) * P)
                    for c in range(2):
                        cols = slice(c * BANK, (c + 1) * BANK)
                        last = product(pS[2 * t + c][:, :], hT_hi[:, rows], hT_lo[:, rows],
                                       two_k(slot_hi(n))[:, ft, cols], two_k(slot_lo(n))[:, ft, cols],
                                       first and ft == 0, final and ft == 1)
                    if final and ft == 1 and t == 0:
                        last.then_inc(first_tile_done, 1)
                last.then_inc(slots_used, 1)

            def dense_step(n0, s, rounds, first=False):
                pe.wait_ge(silu_ready, s + 2 * rounds)
                up_slot(n0, pG, rounds)
                pe.wait_ge(hmul_ready, s + 2 * rounds)
                up_slot(n0 + 1, pU, rounds)
                down_slot(n0 + 2, s - 1, rounds, first=first)

            def dense():
                b = DENSE_BASE
                turn_normed(1)
                pe.wait_ge(xlo_ready, 8)
                up_slot(b, pG, 0)
                up_slot(b + 1, pU, 0)
                for u in range(2):
                    dense_step(b + 2 + 3 * u, 1 + u, 0, first=u == 0)
                with pe.Fori(1, DENSE_STEPS // 2) as r:
                    for u in range(2):
                        dense_step(b + 2 + 3 * u, 1 + u, r)
                down_slot(b + DENSE_SLOTS - 1, DENSE_STEPS - 1, 0, final=True)

            def gather(count):
                pe.wait_ge(pick_ready, count)
                for part, dst in ((hn_hi, (pS[1], pS[2])), (hn_lo, (pS[3], pU))):
                    for q in range(2):
                        for k in range(4):
                            cols = slice((4 * q + k) * P, (4 * q + k + 1) * P)
                            for t in range(NT):
                                last = pe.matmul(dst[q][:, k * P:(k + 1) * P], part[:, t, cols], pick[:, t, :],
                                                 start=t == 0, stop=t == NT - 1)
                        last.then_inc(gathered, 1)

            def route():
                keep_clock(pG, 12)
                turn_normed(3)
                pe.wait_ge(rwlo_ready, 1)
                for k in range(KT):
                    if k % 4 == 0:
                        pe.wait_ge(xlo_ready, 15 + k // 4)
                    last = product(pY0[0:E, 0:SEQ], rw_hi[:, k, :], rw_lo[:, k, :], xT_hi[:, k, :], xT_lo[:, k, :],
                                   k == 0, k == KT - 1)
                last.then_inc(logits_done, 1)
                keep_clock(pG, 2)
                pe.wait_ge(lgT_ready, 1)
                for t in range(NT):
                    last = pe.transpose(pY1[:, t * E:(t + 1) * E], lgT[:, t * P:(t + 1) * P], ident[0:E, 0:E])
                last.then_inc(logits_turned, 1)
                keep_clock(pG, 6)
                pe.wait_ge(sel_ready, 1)
                pe.matmul(pG[:, 0:E], before[:, :], sel[:, 0, :], start=True, stop=True)
                for dst in (pS[0], pY0):
                    pe.matmul(dst[:, 0:E], ones[:, :], sel[:, 0, :], start=True, stop=False)
                for dst, own in ((pS[0], before), (pY0, ones)):
                    pe.matmul(dst[:, 0:E], own[:, :], sel[:, 1, :], start=False, stop=True).then_inc(ranks_done, 1)
                keep_clock(pU, 3)
                pe.wait_ge(hnlo_ready, NT)
                gather(1)

            H0 = DENSE_STEPS

            def item(it):
                B = MOE_BASE

                def up_half(i, k0, dst):
                    pe.wait_ge(lo_ready, B + i + 1 + ITEM * it)
                    for k in range(4):
                        last = token_product(dst[:, :], 0, k0 + k, lambda s: four_k(s)[:, k, :], B + i,
                                             k0 + k == 0, k0 + k == KT - 1)
                    last.then_inc(slots_used, 1)

                def turn_h(c):
                    pe.wait_ge(hmul_ready, H0 + c + 1 + CHUNKS * it)
                    if c == 0:
                        pe.wait_ge(res_added, RES_BASE + 4 * it)
                    else:
                        pe.wait_ge(hlo_ready, H0 + c + CHUNKS * it)
                    for k in range(4):
                        last = pe.transpose(pS[0][:, k * P:(k + 1) * P], hmul[:, k * P:(k + 1) * P], ident[:, :])
                    last.then_inc(h_turned, 1)

                def down(i, c):
                    pe.wait_ge(hlo_ready, H0 + c + 1 + CHUNKS * it)
                    for half in range(2):
                        n = B + i + half
                        pe.wait_ge(lo_ready, n + 1 + ITEM * it)
                        final = c == CHUNKS - 1 and half == 1
                        for kk, d in TILE_LAST if final else K_LAST:
                            k = 2 * half + kk
                            cols = slice(d * BANK, (d + 1) * BANK)
                            last = product(pY[d][:, :], hT_hi[:, k * P:(k + 1) * P], hT_lo[:, k * P:(k + 1) * P],
                                           two_k(slot_hi(n))[:, kk, cols], two_k(slot_lo(n))[:, kk, cols],
                                           c == 0 and k == 0, c == CHUNKS - 1 and k == 3)
                            if final and kk == 1 and d == 0:
                                last.then_inc(y_half_done, 1)
                        last.then_inc(slots_used, 1)

                pe.wait_ge(gxhi_ready, 2 * it + 2)
                pe.wait_ge(gxlo_ready, 2 * it + 2)
                for c in range(CHUNKS):
                    n0 = chunk_slot(c)
                    pe.wait_ge(silu_ready, H0 + c + CHUNKS * it)
                    up_half(n0, 0, pG)
                    if c >= 1:
                        turn_h(c - 1)
                    if c == 1:
                        for t in range(NT):
                            last = pe.transpose(pS[1][:, t * P:(t + 1) * P], pick[:, t, :].bitcast(F32), ident[:, :])
                        last.then_inc(pick_turned, 1)
                    up_half(n0 + 1, 4, pG)
                    pe.wait_ge(hmul_ready, H0 + c + CHUNKS * it)
                    up_half(n0 + 2, 0, pU)
                    up_half(n0 + 3, 4, pU)
                    if c >= 1:
                        down(n0 + 4, c - 1)
                turn_h(CHUNKS - 1)
                pe.wait_ge(pickT_ready, it + 1)
                gather(it + 2)
                down(chunk_slot(CHUNKS), CHUNKS - 1)
                pe.wait_ge(gxhi_ready, 2 * it + 4)
                pe.wait_ge(gxlo_ready, 2 * it + 4)
                for c in range(2):
                    pe.wait_ge(ylo_ready, c + 1 + 2 * it)
                    for t in range(NT):
                        pe.matmul(pS[2 * t + c][:, :], pickT[:, t, :], y_hi[:, 4 * c:4 * c + 4, :],
                                  start=True, stop=False)
                        pe.matmul(pS[2 * t + c][:, :], pickT[:, t, :], y_lo[:, 4 * c:4 * c + 4, :],
                                  start=False, stop=True).then_inc(scattered, 1)

            pe.wait_ge(masks_ready, 1)
            keep_clock(pU, 16)
            mix(0)
            dense()
            mix(1)
            route()
            with pe.Fori(0, E) as it:
                item(it)
            pe.wait_ge(steer_ready, 2)
            extra = pe.value_load(steer[0:1, OVER + 1:OVER + 2], min_val=0, max_val=OVER)
            with pe.Fori(0, OVER) as j:
                with pe.If(extra > j):
                    item(j + E)


def dft_tables(seq, head, per_tile):
    s = np.arange(seq)
    angle = 2 * np.pi * (np.outer(s, s) % seq) / seq
    over_seq = np.concatenate([np.cos(angle), np.sin(angle)], axis=1).astype(np.float32)
    d = np.arange(head)
    angle = 2 * np.pi * (np.outer(d, d) % head) / head
    scale = 1.0 / np.sqrt(seq * head)
    over_head = np.stack([np.kron(np.eye(per_tile), np.cos(angle) * scale),
                          np.kron(np.eye(per_tile), -np.sin(angle) * scale)]).astype(np.float32)
    return over_seq, over_head


_INS = ['x', 'norm_mix_g', 'w_in', 'vnorm_g', 'vnorm_b', 'w_spatial', 'b_spatial', 'conv_w', 'w_out',
        'norm_ffn_g', 'dense_w_gate', 'dense_w_up', 'dense_w_down', 'router_w',
        'moe_w_gate', 'moe_w_up', 'moe_w_down', 'norm_final_g']


def kernel(**inputs):
    import numpy as _np
    import concourse.bacc as _bacc
    from concourse import mybir as _mybir
    from concourse.bass_utils import run_bass_kernel_spmd as _run

    nc = _bacc.Bacc("TRN2", target_bir_lowering=False, num_devices=1)
    arrays, args = {}, []
    data = {name: _np.ascontiguousarray(inputs[name]) for name in _INS}
    seq = data['x'].shape[1]
    w_a = data['w_in'].shape[2] - 2 * data['vnorm_g'].shape[1] - 3 * data['conv_w'].shape[2]
    head = w_a // GROUPS_A
    data['dft_seq'], data['dft_head'] = dft_tables(seq, head, P // head)
    for name, a in data.items():
        arrays[f"in_{name}_dram"] = a
        args.append(nc.dram_tensor(f"in_{name}_dram", a.shape, _mybir.dt.from_np(a.dtype), kind="ExternalInput").ap())
    shape = data['x'].shape
    args.append(nc.dram_tensor("out_0_dram", shape, _mybir.dt.float32, kind="ExternalOutput").ap())
    hybrid_encoder(nc, *args)
    r = _run(nc, [arrays], core_ids=[0])
    return r.results[0]["out_0_dram"]
```

```python
import numpy as np

import concourse.bass as bass
from concourse import mybir
from contextlib import ExitStack

F32 = mybir.dt.float32
F32R = mybir.dt.float32r
I32 = mybir.dt.int32
U32 = mybir.dt.uint32
ALU = mybir.AluOpType
ACT = mybir.ActivationFunctionType
AX = mybir.AxisListType

P = 128
BANK = 512
EPS = 1e-6
TOP_K = 2
GROUPS_A = 4


def hybrid_encoder(nc, x, norm_mix_g, w_in, vnorm_g, vnorm_b, w_spatial, b_spatial, conv_w, w_out,
                   norm_ffn_g, dense_w_gate, dense_w_up, dense_w_down, router_w,
                   moe_w_gate, moe_w_up, moe_w_down, norm_final_g, dft_seq, dft_head, out):
    _, SEQ, D = x.shape
    DEPTH, _, D_IN = w_in.shape
    W_B = vnorm_g.shape[1]
    HEADS_B = b_spatial.shape[2]
    HEAD = W_B // HEADS_B
    TAPS, W_C = conv_w.shape[1:]
    W_A = D_IN - 2 * W_B - 3 * W_C
    F_DENSE = dense_w_gate.shape[2]
    E = router_w.shape[2]
    F_EXP = moe_w_gate.shape[3]
    NT = SEQ // P
    KT = D // P
    TOKEN_COLS = W_A + 2 * W_B
    FEAT_TILES = 3 * W_C // P
    CT = W_C // P
    AT = W_A // P
    BT = W_B // P
    assert NT == 2 and KT == 8 and TOKEN_COLS == 2 * BANK and SEQ == 2 * P and E == 8

    SLOT = 2048
    RAW = 6
    SPLIT = 3
    MIX_IN_TOKEN = 4
    MIX_IN_FEAT = -(-FEAT_TILES // 2)
    MIX_IN = MIX_IN_TOKEN + MIX_IN_FEAT
    MIX_OUT = KT // 2
    MIX_SLOTS = MIX_IN + MIX_OUT
    DENSE_STEPS = F_DENSE // (2 * P)
    DENSE_SLOTS = 3 * DENSE_STEPS
    CHUNKS = F_EXP // BANK
    ITEM = 6 * CHUNKS
    EXTRA = 8
    DEEP = RAW + EXTRA
    MIX_BASE = [0, MIX_SLOTS + DENSE_SLOTS]
    DENSE_BASE = MIX_SLOTS
    MOE_BASE = 2 * MIX_SLOTS + DENSE_SLOTS
    assert ITEM % SPLIT == 0 and ITEM % DEEP == 0 and DENSE_STEPS % 2 == 1

    OVER = (TOP_K * SEQ) // (P + 1)
    ITEMS = E + OVER
    TAB = 8
    RANK, SEL, GATE, EID = 0, 2, 4, 6
    RES_BASE = 3 * 4

    ctx = ExitStack()
    with ctx:
        def sb(name, shape, dt=F32):
            return ctx.enter_context(nc.sbuf_tensor(name, shape, dt))

        def sem(name):
            return ctx.enter_context(nc.semaphore(name))

        raw = sb("raw", [P, RAW, SLOT])
        w_hi = sb("w_hi", [P, SPLIT, SLOT], F32R)
        w_lo = sb("w_lo", [P, SPLIT, SLOT], F32R)
        h = sb("h", [P, NT, D])
        hn = sb("hn", [P, NT, D])
        xT_hi = sb("xT_hi", [P, KT, SEQ], F32R)
        xT_lo = sb("xT_lo", [P, KT, SEQ], F32R)
        late = sb("late", [P, EXTRA - 2, SLOT])

        def flat_late(slot, start, size):
            return late[:, slot:, :].rearrange("p x n -> p (x n)")[:, start:start + size]

        def in_late(slot, start, a, b):
            return flat_late(slot, start, a * b).rearrange("p (a b) -> p a b", a=a)

        cs = in_late(0, 0, NT, 2 * SEQ)
        bd = in_late(0, NT * 2 * SEQ, 2, P)
        vg_bc = in_late(0, NT * 2 * SEQ + 2 * P, DEPTH, W_B)
        wsT = in_late(1, 0, DEPTH * HEADS_B, P)
        uv_t = in_late(2, 0, NT, 2 * W_B)
        feat = in_late(3, 0, FEAT_TILES, SEQ)
        ws_raw = in_late(3, 0, DEPTH * HEADS_B, P)
        pad = in_late(3, FEAT_TILES * SEQ, CT, SEQ + 2)
        vb_bc = in_late(3, FEAT_TILES * SEQ + CT * (SEQ + 2), DEPTH, W_B)
        rw = in_late(1, DEPTH * HEADS_B * P, KT, E)
        sg = sb("sg", [P, BANK])
        dft1 = [sg[:, :], flat_late(2, NT * 2 * W_B, BANK)]
        ident = sb("ident", [P, P])
        before = flat_late(5, D, P)
        ones = flat_late(5, D + P, P)
        iota = sb("iota", [P, P])
        one_row = sb("one_row", [P, E])
        gain0 = sb("gain0", [P, D])
        gain1 = flat_late(5, 0, D)
        gain = [gain0[:, :], gain1]
        small = D + 2 * P
        bs = in_late(5, small, DEPTH, HEADS_B)
        cw = in_late(5, small + DEPTH * HEADS_B, DEPTH, TAPS * CT)
        small += DEPTH * (HEADS_B + TAPS * CT)
        hmul = sb("hmul", [P, BANK])
        a_sb = hmul[:, :].rearrange("p (t c) -> p t c", t=NT)
        assert NT * W_A == BANK
        hT_hi = sb("hT_hi", [P, BANK], F32R)
        hT_lo = sb("hT_lo", [P, BANK], F32R)
        y_hi, y_lo = xT_hi[:, :, P:2 * P], xT_lo[:, :, P:2 * P]
        pick = sb("pick", [P, NT, P])
        pickT = sb("pickT", [P, NT, P], F32R)
        rw_hi, rw_lo = (pickT[:, i, 0:KT * E].rearrange("p (k e) -> p k e", k=KT) for i in range(2))
        tab = sb("tab", [P, ITEMS + 2, TAB])
        cur = sb("cur", [P, 2, TAB])
        stat = sb("stat", [P, 4, 2 * (DEPTH * 2 + 1)])
        bn = in_late(5, small, DEPTH * NT, 6)
        mv = in_late(5, small + 6 * DEPTH * NT, DEPTH * NT, 2)
        vst = in_late(5, small + 8 * DEPTH * NT, 3, DEPTH * NT)
        eps_c = sb("eps_c", [P, 1])
        topi = sb("topi", [P, NT, E], U32)
        places = np.cumsum([0, NT * E, NT * E, NT * E, NT * E, 2 * NT * E, 2 * E, OVER * E, OVER * TAB * E]).tolist()
        lg, top, topf, sel, oh, over, ohj, prod = (hmul[:, a:b].rearrange("p (t e) -> p t e", e=E)
                                                   for a, b in zip(places, places[1:]))
        rt = hmul[:, places[-1]:places[-1] + 4 * NT].rearrange("p (r t) -> p r t", r=4)
        lgT = sg[0:E, 0:SEQ]
        assert places[-1] + 4 * NT <= BANK
        steer = sb("steer", [1, OVER + 2], I32)

        with nc.sbuf_tensor("mixT_hi", [P, KT, SEQ], F32R) as mixT_hi, \
                nc.sbuf_tensor("mixT_lo", [P, KT, SEQ], F32R) as mixT_lo:
            pass
        late_mix = sb("late_mix", [P, 2, SLOT])

        banks = [ctx.enter_context(nc.psum_tensor(n, [P, BANK], F32))
                 for n in ("pG", "pU", "pY0", "pY1", "pS0", "pS1", "pS2", "pS3")]
        pG, pU, pY0, pY1, *pS = banks
        pY = [pY0, pY1]
        FEAT_BANK = [pG, pU, pY0, pY1, pG]
        GATHER_BANK = [pS[1], pU]
        OUT_BANK = [pS[2], pS[3], pU, pY0]

        slot_loaded = [sem(f"slot_loaded{i}") for i in range(RAW)]
        expert_loaded = [sem(f"expert_loaded{i}") for i in range(DEEP)]
        hi_ready, lo_ready, slots_used = sem("hi_ready"), sem("lo_ready"), sem("slots_used")
        x_loaded = [sem(f"x_loaded{t}") for t in range(NT)]
        column_loaded = sem("column_loaded")
        ws_loaded, dft_loaded, row_loaded, rw_loaded = (sem("ws_loaded"), sem("dft_loaded"),
                                                        sem("row_loaded"), sem("rw_loaded"))
        g0_loaded = sem("g0_loaded")
        g_loaded = [sem(f"g_loaded{i}") for i in range(2)]
        eps_set = sem("eps_set")
        masks_set, masks_ready = sem("masks_set"), sem("masks_ready")
        ws_turned, wsT_ready = sem("ws_turned"), sem("wsT_ready")
        sq_ready, root_ready, inv_ready, hn_ready = (sem("sq_ready"), sem("root_ready"),
                                                               sem("inv_ready"), sem("hn_ready"))
        hn_turned, xhi_ready, xlo_ready = sem("hn_turned"), sem("xhi_ready"), sem("xlo_ready")
        a_ready, uv_ready, feat_ready = sem("a_ready"), sem("uv_ready"), sem("feat_ready")
        dft1_done, dft1_ready, dft2_done = sem("dft1_done"), sem("dft1_ready"), sem("dft2_done")
        ln_step, ln_root, vn_ready = sem("ln_step"), sem("ln_root"), sem("vn_ready")
        z_done, g_ready, g_turned = sem("z_done"), sem("g_ready"), sem("g_turned")
        conv_step, y_ready = sem("conv_step"), sem("y_ready")
        mixhi_ready, mixlo_ready = sem("mixhi_ready"), sem("mixlo_ready")
        res_added, first_tile_done = sem("res_added"), sem("first_tile_done")
        silu_ready, hmul_ready, h_turned, hhi_ready, hlo_ready = (sem("silu_ready"), sem("hmul_ready"), sem("h_turned"),
                                                                  sem("hhi_ready"), sem("hlo_ready"))
        rwhi_ready, rwlo_ready, logits_done = sem("rwhi_ready"), sem("rwlo_ready"), sem("logits_done")
        lgT_ready, logits_turned = sem("lgT_ready"), sem("logits_turned")
        route_step, diff_ready, exp_ready, sel_ready, ranks_done, steer_ready = (
            sem("route_step"), sem("diff_ready"), sem("exp_ready"), sem("sel_ready"), sem("ranks_done"),
            sem("steer_ready"))
        cur_ready, pick_ready, pick_turned, pickT_ready = (sem("cur_ready"), sem("pick_ready"), sem("pick_turned"),
                                                           sem("pickT_ready"))
        gathered, gxhi_ready, gxlo_ready = sem("gathered"), sem("gxhi_ready"), sem("gxlo_ready")
        y_half_done = sem("y_half_done")
        yhi_ready, ylo_ready, scattered, stored = sem("yhi_ready"), sem("ylo_ready"), sem("scattered"), sem("stored")

        block = ctx.enter_context(nc.Block())

        def four_k(s):
            return s.rearrange("p (k n) -> p k n", n=BANK)

        def eight_k(s, n=2 * P):
            return s[:, 0:KT * n].rearrange("p (k n) -> p k n", n=n)

        def two_k(s):
            return s.rearrange("p (k n) -> p k n", n=D)

        deep_ring = ([late[:, p, :] for p in range(3)] + [raw[:, (MOE_BASE + p) % RAW, :] for p in range(3)] +
                     [late[:, p, :] for p in range(3, 5)] + [raw[:, (MOE_BASE + p) % RAW, :] for p in range(3, RAW)] +
                     [late_mix[:, p, :] for p in range(2)] + [late[:, 5, :]])
        assert len(deep_ring) == DEEP

        def slot_raw(n):
            if n < MOE_BASE:
                return raw[:, n % RAW, :]
            return deep_ring[(n - MOE_BASE) % DEEP]

        def wait_loaded(engine, n, it, per):
            if n < MOE_BASE:
                engine.wait_ge(slot_loaded[n % RAW], 16 * (n // RAW + 1) + 16 * (per // RAW) * it)
            else:
                rnd, place = divmod(n - MOE_BASE, DEEP)
                engine.wait_ge(expert_loaded[place], 16 * (rnd + 1) + 16 * (per // DEEP) * it)

        def slot_hi(n):
            return w_hi[:, n % SPLIT, :]

        def slot_lo(n):
            return w_lo[:, n % SPLIT, :]

        K_LAST = [(0, 0), (0, 1), (1, 0), (1, 1)]
        TILE_LAST = [(0, 0), (1, 0), (0, 1), (1, 1)]

        def chunk_slot(c):
            return 6 * c - 2 if c else 0

        @block.sync
        def _(sp):
            for t in range(NT):
                sp.dma_start(h[:, t, :], x[0, t * P:(t + 1) * P, :]).then_inc(x_loaded[t], 16)
                if t == 0:
                    sp.dma_start(gain[0], norm_mix_g[0:1, :].to_broadcast([P, D])).then_inc(g0_loaded, 16)

            def load(n, view, src, rounds=0):
                if n >= RAW:
                    sp.wait_ge(lo_ready, n - RAW + 1 + RAW * rounds)
                sp.dma_start(view(slot_raw(n)), src).then_inc(slot_loaded[n % RAW], 16)

            def small_loads(i):
                if i == 2:
                    sp.dma_start(ws_raw, w_spatial.rearrange("l h p q -> p (l h) q")).then_inc(ws_loaded, 16)
                if i == 3:
                    sp.dma_start(cs[:, :, :], dft_seq.rearrange("(t p) n -> p t n", p=P)).then_inc(dft_loaded, 16)
                    sp.dma_start(bd[:, :, :], dft_head.rearrange("c p n -> p c n")).then_inc(dft_loaded, 16)
                if i == MIX_IN_TOKEN:
                    for layer in range(DEPTH):
                        sp.dma_start(vg_bc[:, layer, :], vnorm_g[layer:layer + 1, :].to_broadcast([P, W_B])) \
                            .then_inc(row_loaded, 16)
                        sp.dma_start(vb_bc[:, layer, :], vnorm_b[layer:layer + 1, :].to_broadcast([P, W_B])) \
                            .then_inc(row_loaded, 16)

            def mix_loads(layer):
                b = MIX_BASE[layer]
                w = w_in[layer].rearrange("(k p) n -> p k n", p=P)
                for i in range(MIX_IN_TOKEN):
                    if layer == 0:
                        small_loads(i)
                    j, kh = i // 2, i % 2
                    load(b + i, four_k, w[:, 4 * kh:4 * kh + 4, j * BANK:(j + 1) * BANK])
                if layer == 0:
                    small_loads(MIX_IN_TOKEN)
                for i in range(MIX_IN_FEAT):
                    c0 = TOKEN_COLS + 2 * P * i
                    n = min(2 * P, D_IN - c0)
                    load(b + MIX_IN_TOKEN + i, lambda s: eight_k(s, n), w[:, :, c0:c0 + n])
                w = w_out[layer].rearrange("(k p) n -> p k n", p=P)
                for i in range(MIX_OUT):
                    if layer == 1 and i >= 1:
                        item_load(i - 1, 0, None)
                    load(b + MIX_IN + i, two_k, w[:, 2 * i:2 * i + 2, :])

            def dense_load(n, w, s, rounds=0):
                if w is dense_w_down:
                    view, src = two_k, w[0].rearrange("(f p) n -> p f n", p=P)[:, bass.ds(2 * s, 2), :]
                else:
                    view, src = eight_k, w[0].rearrange("(k p) n -> p k n", p=P)[:, :, bass.ds(2 * P * s, 2 * P)]
                load(n, view, src, rounds)

            def experts_load(i, view, src, it):
                place = i % DEEP
                if it is not None:
                    sp.wait_ge(lo_ready, MOE_BASE + i - DEEP + 1 + ITEM * it)
                elif place == 0:
                    sp.wait_ge(dft2_done, DEPTH)
                    sp.wait_ge(vn_ready, 2 * NT * DEPTH)
                elif place == 1:
                    sp.wait_ge(z_done, NT * DEPTH)
                elif place == 2:
                    sp.wait_ge(g_turned, 2 * DEPTH)
                elif place < 6:
                    sp.wait_ge(lo_ready, MOE_BASE - RAW + place - 3 + 1)
                elif place == 6:
                    sp.wait_ge(mixlo_ready, (3 + CT) * DEPTH)
                elif 8 <= place < 11:
                    sp.wait_ge(lo_ready, MOE_BASE - RAW + place - 5 + 1)
                elif place == 11:
                    sp.wait_ge(slots_used, MOE_BASE)
                elif place == 13:
                    sp.wait_ge(ranks_done, 2)
                sp.dma_start(view(slot_raw(MOE_BASE + i)), src).then_inc(expert_loaded[place], 16)

            def item_load(i, expert, it):
                def of(e):
                    return bass.ds(e, 1)

                c = 0 if i < 4 else (i + 2) // 6
                k = i - chunk_slot(c)
                if i >= chunk_slot(CHUNKS):
                    c, k = CHUNKS, i - chunk_slot(CHUNKS) + 4
                if k < 4:
                    w = moe_w_gate if k < 2 else moe_w_up
                    src = w[0, of(expert), (k % 2) * D // 2:(k % 2 + 1) * D // 2, c * BANK:(c + 1) * BANK]
                    experts_load(i, four_k, src.rearrange("o (k p) n -> p (o k) n", p=P), it)
                else:
                    f0 = (c - 1) * BANK + (k - 4) * 2 * P
                    src = moe_w_down[0, of(expert), f0:f0 + 2 * P, :]
                    experts_load(i, two_k, src.rearrange("o (f p) n -> p (o f) n", p=P), it)

            mix_loads(0)
            dense_load(DENSE_BASE, dense_w_gate, 0)
            dense_load(DENSE_BASE + 1, dense_w_up, 0)
            with sp.Fori(0, DENSE_STEPS // 2) as r:
                for u in range(2):
                    n0 = DENSE_BASE + 2 + 3 * u
                    dense_load(n0, dense_w_gate, 2 * r + 1 + u, r)
                    dense_load(n0 + 1, dense_w_up, 2 * r + 1 + u, r)
                    dense_load(n0 + 2, dense_w_down, 2 * r + u, r)
            dense_load(DENSE_BASE + DENSE_SLOTS - 1, dense_w_down, DENSE_STEPS - 1)
            mix_loads(1)

            for i in range(MIX_OUT - 1, DEEP):
                item_load(i, 0, None)
            with sp.Fori(0, E - 1) as it:
                for i in range(DEEP, ITEM):
                    item_load(i, it, it)
                for i in range(DEEP):
                    item_load(i, it + 1, it + 1)
            for i in range(DEEP, ITEM):
                item_load(i, E - 1, E - 1)
            sp.wait_ge(steer_ready, 2)
            extra = sp.value_load(steer[0:1, OVER + 1:OVER + 2], min_val=0, max_val=OVER)
            with sp.Fori(0, OVER) as j:
                with sp.If(extra > j):
                    mine = sp.value_load(steer[0:1, bass.ds(j, 1)], min_val=0, max_val=E - 1)
                    for i in range(ITEM):
                        item_load(i, mine, j + E)
            for t in range(NT):
                sp.wait_ge(hn_ready, 4 * 2 * DEPTH + 2 * t + 2)
                sp.dma_start(out[0, t * P:(t + 1) * P, :], hn[:, t, :]).then_inc(stored, 16)
            sp.wait_ge(stored, 16 * NT)

        @block.gpsimd
        def _(pool):
            gains = [None, norm_ffn_g[0:1, :], norm_mix_g[1:2, :], norm_ffn_g[1:2, :],
                     norm_final_g.rearrange("(o n) -> o n", o=1)]

            def load_gain(m):
                pool.dma_start(gain[m % 2], gains[m].to_broadcast([P, D])).then_inc(g_loaded[m % 2], 16)

            pool.memset(eps_c[:, :], EPS).then_inc(eps_set, 1)
            pool.memset(ident[:, :], 0.0).then_inc(masks_set, 1)
            pool.wait_ge(masks_set, 1)
            pool.affine_select(out=ident[:, :], in_=ident[:, :], compare_op=ALU.not_equal, fill=1.0, base=0,
                               pattern=[[-1, P]], channel_multiplier=1).then_inc(masks_ready, 1)
            pool.memset(ones[:, :], 1.0).then_inc(masks_set, 1)
            pool.wait_ge(masks_set, 2)
            pool.affine_select(out=before[:, :], in_=ones[:, :], compare_op=ALU.is_gt, fill=0.0, base=0,
                               pattern=[[1, P]], channel_multiplier=-1).then_inc(masks_ready, 1)
            pool.memset(one_row[:, :], 1.0).then_inc(masks_ready, 1)
            pool.memset(pad[:, :, 0:1], 0.0).then_inc(masks_ready, 1)
            pool.memset(pad[:, :, SEQ + 1:SEQ + 2], 0.0).then_inc(masks_ready, 1)
            pool.iota(iota[:, :], pattern=[[1, P]], base=0, channel_multiplier=0,
                      allow_small_or_imprecise_dtypes=True).then_inc(masks_ready, 1)
            pool.memset(tab[:, :, :], 0.0).then_inc(masks_ready, 1)
            pool.wait_ge(slots_used, 1)
            for layer in range(DEPTH):
                pool.dma_start(bs[:, layer, :], b_spatial[layer]).then_inc(column_loaded, 16)
                for tap in range(TAPS):
                    pool.dma_start(cw[:, layer, tap * CT:(tap + 1) * CT],
                                   conv_w[layer, tap, :].rearrange("(f p) -> p f", p=P),
                                   allow_slow_non_contiguous=True).then_inc(column_loaded, 16)
            load_gain(1)
            pool.dma_start(rw[:, :, :], router_w[0].rearrange("(k p) e -> p k e", p=P)).then_inc(rw_loaded, 16)
            for m in range(2, len(gains)):
                pool.wait_ge(hn_ready, 4 * (m - 2) + 4)
                load_gain(m)

        MASKS = 7

        @block.scalar
        def _(act):
            def split(n, it=0, per=ITEM):
                wait_loaded(act, n, it, per)
                if n >= SPLIT:
                    act.wait_ge(slots_used, n - SPLIT + 1 + per * it)
                act.activation(slot_hi(n), slot_raw(n), ACT.Copy).then_inc(hi_ready, 1)

            def split_half(n):
                act.wait_ge(slot_loaded[n % RAW], 16 * (n // RAW + 1))
                act.wait_ge(slots_used, n - SPLIT + 1)
                act.activation(slot_hi(n)[:, 0:KT * P], raw[:, n % RAW, 0:KT * P], ACT.Copy).then_inc(hi_ready, 1)

            def roots(m, wait):
                for t in range(NT):
                    k = 2 * m + t
                    wait(t)
                    act.activation(hn[:, t, :], h[:, t, :], ACT.Square, accum_out=stat[:, 0, k:k + 1]).then_inc(sq_ready, 1)
                    act.wait_ge(sq_ready, k + 1)
                    act.activation(stat[:, 1, k:k + 1], stat[:, 0, k:k + 1], ACT.Sqrt, bias=eps_c[:, 0:1],
                                   scale=1.0 / D).then_inc(root_ready, 1)

            def norm(m):
                def wait(t):
                    if m == 0:
                        act.wait_ge(x_loaded[t], 16)
                    else:
                        act.wait_ge(res_added, 4 * (m - 1) + 2 * (t + 1))
                        act.wait_ge(hn_ready, 4 * m)
                if m == 0:
                    act.wait_ge(eps_set, 1)
                act.activation(stat[:, 3, 0:1], eps_c[:, 0:1], ACT.Sqrt)
                roots(m, wait)
                for t in range(NT):
                    for q in range(2):
                        act.wait_ge(hn_turned, 4 * m + 2 * t + q + 1)
                        act.activation(xT_hi[:, 4 * q:4 * q + 4, t * P:(t + 1) * P],
                                       pS[2 * t + q][:, :].rearrange("p (k s) -> p k s", k=4),
                                       ACT.Copy).then_inc(xhi_ready, 1)
                    if m == 0 and t == 0:
                        split(0)

            def mix(layer):
                b = MIX_BASE[layer]
                f = b + MIX_IN_TOKEN
                norm(2 * layer)
                if layer == 0:
                    split(1)
                for n in range(b + 2, b + MIX_SLOTS + 2):
                    if n == f + MIX_IN_FEAT - 1:
                        split_half(n)
                    else:
                        split(n)
                    if n == b + 4:
                        act.wait_ge(slots_used, b + 2)
                        for t in range(NT):
                            act.activation(a_sb[:, t, :], pS[t][:, 0:W_A], ACT.Copy).then_inc(a_ready, 1)
                        for t in range(NT):
                            act.activation(uv_t[:, t, 0:BANK - W_A], pS[t][:, W_A:BANK],
                                           ACT.Gelu_apprx_tanh).then_inc(uv_ready, 1)
                    if n == b + 6:
                        act.wait_ge(slots_used, b + 4)
                        for t in range(NT):
                            act.activation(uv_t[:, t, BANK - W_A:2 * W_B], pS[2 + t][:, :],
                                           ACT.Gelu_apprx_tanh).then_inc(uv_ready, 1)
                        for t in range(NT):
                            act.wait_ge(ln_step, 5 * (NT * layer + t) + 3)
                            k = NT * layer + t
                            act.activation(vst[:, 1, k:k + 1], vst[:, 0, k:k + 1], ACT.Sqrt).then_inc(ln_root, 1)
                    i = n - f - SPLIT
                    if 0 <= i < MIX_IN_FEAT:
                        act.wait_ge(slots_used, f + i + 1)
                        w = min(2, FEAT_TILES - 2 * i)
                        act.activation(feat[:, 2 * i:2 * i + w, :],
                                       FEAT_BANK[i][:, 0:w * SEQ].rearrange("p (f s) -> p f s", f=w),
                                       ACT.Copy).then_inc(feat_ready, 1)
                    if n == f + 4:
                        act.wait_ge(dft2_done, layer + 1)
                        act.activation(mixT_hi[:, 0:AT, :], pS[0][:, :].rearrange("p (k s) -> p k s", k=AT),
                                       ACT.Copy).then_inc(mixhi_ready, 1)
                    if n == f + 6:
                        act.wait_ge(g_turned, 2 * layer + 1)
                        act.activation(mixT_hi[:, AT:AT + 2, :], pS[1][:, :].rearrange("p (k s) -> p k s", k=2),
                                       ACT.Copy).then_inc(mixhi_ready, 1)
                        act.wait_ge(g_turned, 2 * layer + 2)
                        act.activation(mixT_hi[:, AT + 2, :], pS[0][:, 0:SEQ], ACT.Copy).then_inc(mixhi_ready, 1)
                    if n == b + 11:
                        for ft in range(CT):
                            act.wait_ge(y_ready, CT * layer + ft + 1)
                            act.activation(mixT_hi[:, AT + BT + ft, :], feat[:, ft, :],
                                           ACT.Copy).then_inc(mixhi_ready, 1)

            def dense_step(n0, s, rounds=0):
                it = dict(it=rounds, per=RAW)
                split(n0 + 2, **it)
                act.wait_ge(slots_used, n0 + 1 + RAW * rounds)
                act.wait_ge(hmul_ready, s + 2 * rounds)
                act.activation(sg[:, :], pG[:, :], ACT.Silu).then_inc(silu_ready, 1)
                split(n0 + 3, **it)
                split(n0 + 4, **it)
                act.wait_ge(hmul_ready, s + 1 + 2 * rounds)
                act.wait_ge(slots_used, n0 + 3 + RAW * rounds)
                act.activation(hT_hi[:, :], hmul[:, :], ACT.Copy).then_inc(hhi_ready, 1)

            def dense():
                norm(1)
                b = DENSE_BASE
                split(b + 2)
                act.wait_ge(slots_used, b + 1)
                act.activation(sg[:, :], pG[:, :], ACT.Silu).then_inc(silu_ready, 1)
                split(b + 3)
                act.wait_ge(hmul_ready, 1)
                act.activation(hT_hi[:, :], hmul[:, :], ACT.Copy).then_inc(hhi_ready, 1)
                with act.Fori(0, DENSE_STEPS // 2) as r:
                    for u in range(2):
                        dense_step(b + 2 + 3 * u, 1 + u, r)
                split(b + DENSE_SLOTS + 1)

            def evacuate_gather(g, halves=(0, 1)):
                for q in halves:
                    act.wait_ge(gathered, 2 * g + q + 1)
                    act.activation(xT_hi[:, 4 * q:4 * q + 4, 0:P],
                                   GATHER_BANK[q][:, :].rearrange("p (k s) -> p k s", k=4),
                                   ACT.Copy).then_inc(gxhi_ready, 1)

            def first_slots(it):
                evacuate_gather(it)
                for i in range(SPLIT):
                    split(MOE_BASE + i, it)

            def route():
                norm(3)
                split(MOE_BASE + 2)
                act.activation(stat[:, 3, 0:1], eps_c[:, 0:1], ACT.Exp)
                act.wait_ge(diff_ready, 1)
                act.activation(rt[:, 1, :], rt[:, 0, :], ACT.Exp).then_inc(exp_ready, 1)
                evacuate_gather(0)

            H0 = DENSE_STEPS

            def item(it, ahead):
                B = MOE_BASE
                act.activation(stat[:, 3, 0:1], eps_c[:, 0:1], ACT.Silu)
                for c in range(CHUNKS):
                    n0 = chunk_slot(c)
                    done = H0 + c + CHUNKS * it
                    if c >= 1:
                        split(B + n0 + 2, it)
                        act.wait_ge(h_turned, c + CHUNKS * it)
                        act.wait_ge(slots_used, B + n0 + ITEM * it)
                        act.activation(hT_hi[:, :], pS[0][:, :], ACT.Copy).then_inc(hhi_ready, 1)
                    split(B + n0 + 3, it)
                    act.wait_ge(slots_used, B + n0 + 2 + ITEM * it)
                    act.wait_ge(hmul_ready, done)
                    act.activation(sg[:, :], pG[:, :], ACT.Silu).then_inc(silu_ready, 1)
                    split(B + n0 + 4, it)
                    split(B + n0 + 5, it)
                    if c >= 1:
                        split(B + n0 + 6, it)
                        split(B + n0 + 7, it)
                    if c == 2:
                        act.wait_ge(pick_turned, it + 1)
                        act.activation(pickT[:, :, :], pS[1][:, 0:NT * P].rearrange("p (t s) -> p t s", t=NT),
                                       ACT.Copy).then_inc(pickT_ready, 1)
                act.wait_ge(h_turned, CHUNKS + CHUNKS * it)
                act.activation(hT_hi[:, :], pS[0][:, :], ACT.Copy).then_inc(hhi_ready, 1)
                if ahead:
                    split(B + ITEM, it)
                    evacuate_gather(it + 1, halves=[0])
                    split(B + ITEM + 1, it)
                for c in range(2):
                    if c == 0:
                        act.wait_ge(y_half_done, it + 1)
                    else:
                        act.wait_ge(slots_used, B + ITEM + ITEM * it)
                    act.activation(y_hi[:, 4 * c:4 * c + 4, :], pY[c][:, :].rearrange("p (k s) -> p k s", k=4),
                                   ACT.Copy).then_inc(yhi_ready, 1)
                if ahead:
                    split(B + ITEM + 2, it)
                    evacuate_gather(it + 1, halves=[1])

            mix(0)
            dense()
            act.wait_ge(rw_loaded, 16)
            act.activation(rw_hi, rw[:, :, :], ACT.Copy).then_inc(rwhi_ready, 1)
            mix(1)
            route()
            with act.Fori(0, E - 1) as it:
                item(it, True)
            item(E - 1, False)
            act.wait_ge(steer_ready, 2)
            extra = act.value_load(steer[0:1, OVER + 1:OVER + 2], min_val=0, max_val=OVER)
            with act.Fori(0, OVER) as j:
                with act.If(extra > j):
                    first_slots(j + E)
                    item(j + E, False)
            act.activation(stat[:, 3, 0:1], eps_c[:, 0:1], ACT.Sqrt)
            act.wait_ge(res_added, RES_BASE + 4 * E + 4 * extra)
            roots(4, lambda t: None)

        @block.vector
        def _(dve):
            def split(n, it=0, per=ITEM):
                dve.wait_ge(hi_ready, n + 1 + per * it)
                dve.tensor_tensor(slot_lo(n), slot_raw(n), slot_hi(n).bitcast(F32),
                                  ALU.subtract).then_inc(lo_ready, 1)

            def split_half(n):
                dve.wait_ge(hi_ready, n + 1)
                dve.tensor_tensor(slot_lo(n)[:, 0:KT * P], raw[:, n % RAW, 0:KT * P],
                                  slot_hi(n)[:, 0:KT * P].bitcast(F32), ALU.subtract).then_inc(lo_ready, 1)

            def norm(m, turned=True):
                for t in range(NT):
                    k = 2 * m + t
                    dve.wait_ge(root_ready, k + 1)
                    dve.reciprocal(stat[:, 2, k:k + 1], stat[:, 1, k:k + 1]).then_inc(inv_ready, 1)
                    dve.wait_ge(inv_ready, k + 1)
                    if m == 0:
                        dve.wait_ge(g0_loaded, 16)
                    else:
                        dve.wait_ge(g_loaded[m % 2], 16 * ((m + 1) // 2))
                    for q in range(2):
                        cols = slice(q * BANK, (q + 1) * BANK)
                        dve.scalar_tensor_tensor(out=hn[:, t, cols], in0=h[:, t, cols], scalar=stat[:, 2, k:k + 1],
                                                 in1=gain[m % 2][:, cols], op0=ALU.mult,
                                                 op1=ALU.mult).then_inc(hn_ready, 1)
                if not turned:
                    return
                for t in range(NT):
                    if m == 0 and t == 1:
                        split(0)
                    for q in range(2):
                        n = 4 * m + 2 * t + q
                        hi = xT_hi[:, 4 * q:4 * q + 4, t * P:(t + 1) * P].bitcast(F32)
                        dve.wait_ge(xhi_ready, n + 1)
                        dve.tensor_tensor(xT_lo[:, 4 * q:4 * q + 4, t * P:(t + 1) * P],
                                          pS[2 * t + q][:, :].rearrange("p (k s) -> p k s", k=4), hi,
                                          ALU.subtract).then_inc(xlo_ready, 1)

            def add_residual(products, wait, first):
                for t in range(NT):
                    for c in range(2):
                        wait(2 * t + c)
                        if first is not None:
                            dve.wait_ge(res_added, first)
                        dve.tensor_tensor(h[:, t, c * BANK:(c + 1) * BANK], products[2 * t + c][:, :],
                                          h[:, t, c * BANK:(c + 1) * BANK], ALU.add).then_inc(res_added, 1)

            def finished(q, m, used):
                if q < 2:
                    dve.wait_ge(first_tile_done, m + 1)
                else:
                    dve.wait_ge(slots_used, used)

            def mix_lo_of(dst, src, hi, count):
                dve.wait_ge(mixhi_ready, count)
                dve.tensor_tensor(dst, src, hi.bitcast(F32), ALU.subtract).then_inc(mixlo_ready, 1)

            def mix(layer):
                b = MIX_BASE[layer]
                f = b + MIX_IN_TOKEN
                pieces = (3 + CT) * layer
                norm(2 * layer)
                split(b + 1)
                for n in range(b + 2, b + MIX_SLOTS + 1):
                    if n == f + MIX_IN_FEAT - 1:
                        split_half(n)
                    else:
                        split(n)
                    if layer == 0 and n == b + 4:
                        for i in range(3):
                            dve.wait_ge(ws_turned, i + 1)
                            last = dve.tensor_copy(wsT[:, 4 * i:4 * i + 4, :],
                                                   banks[i][:, :].rearrange("p (h q) -> p h q", h=4))
                        last.then_inc(wsT_ready, 1)
                    if n == b + 6:
                        dve.wait_ge(row_loaded, 16 * DEPTH * 2)
                        dve.wait_ge(column_loaded, 16 * DEPTH * (1 + TAPS))
                        for t in range(NT):
                            k = NT * layer + t
                            s = 5 * k
                            v = uv_t[:, t, W_B:2 * W_B]
                            dve.wait_ge(uv_ready, 4 * layer + 3 + t)
                            dve.bn_stats(bn[:, k, :], v).then_inc(ln_step, 1)
                            dve.wait_ge(ln_step, s + 1)
                            dve.bn_aggr(mv[:, k, :], bn[:, k, :]).then_inc(ln_step, 1)
                            dve.wait_ge(ln_step, s + 2)
                            dve.tensor_scalar(vst[:, 0, k:k + 1], mv[:, k, 1:2], EPS, None,
                                              ALU.add).then_inc(ln_step, 1)
                            dve.wait_ge(ln_root, k + 1)
                            dve.reciprocal(vst[:, 2, k:k + 1], vst[:, 1, k:k + 1]).then_inc(ln_step, 1)
                            dve.wait_ge(ln_step, s + 4)
                            dve.tensor_scalar(v, v, mv[:, k, 0:1], vst[:, 2, k:k + 1], ALU.subtract,
                                              ALU.mult).then_inc(ln_step, 1)
                            dve.wait_ge(ln_step, s + 5)
                            dve.tensor_tensor(v, v, vg_bc[:, layer, :], ALU.mult).then_inc(vn_ready, 1)
                            dve.wait_ge(vn_ready, 2 * k + 1)
                            dve.tensor_tensor(v, v, vb_bc[:, layer, :], ALU.add).then_inc(vn_ready, 1)
                    if n == f + 3:
                        for g in range(AT):
                            dve.wait_ge(dft1_done, AT * layer + g + 1)
                            dve.tensor_copy(dft1[g], pS[g][:, :]).then_inc(dft1_ready, 1)
                    if n == f + 4:
                        mix_lo_of(mixT_lo[:, 0:AT, :], pS[0][:, :].rearrange("p (k s) -> p k s", k=AT),
                                  mixT_hi[:, 0:AT, :], pieces + 1)
                    if n == f + 5:
                        for t in range(NT):
                            dve.wait_ge(z_done, NT * layer + t + 1)
                            for hd in range(HEADS_B):
                                cols = slice(hd * HEAD, (hd + 1) * HEAD)
                                last = dve.scalar_tensor_tensor(
                                    out=uv_t[:, t, cols], in0=pS[2 + t][:, cols], scalar=bs[:, layer, hd:hd + 1],
                                    in1=uv_t[:, t, cols], op0=ALU.add, op1=ALU.mult)
                            last.then_inc(g_ready, 1)
                    if n == f + 6:
                        mix_lo_of(mixT_lo[:, AT:AT + 2, :], pS[1][:, :].rearrange("p (k s) -> p k s", k=2),
                                  mixT_hi[:, AT:AT + 2, :], pieces + 2)
                        mix_lo_of(mixT_lo[:, AT + 2, :], pS[0][:, 0:SEQ], mixT_hi[:, AT + 2, :], pieces + 3)
                    if n == b + 11:
                        dve.wait_ge(feat_ready, MIX_IN_FEAT * (layer + 1))
                        dve.wait_ge(masks_ready, MASKS)
                        step = 4 * layer
                        acc = feat[:, CT:2 * CT, :]
                        dve.tensor_tensor(pad[:, :, 1:SEQ + 1], acc, feat[:, 2 * CT:3 * CT, :],
                                          ALU.mult).then_inc(conv_step, 1)
                        dve.wait_ge(conv_step, step + 1)
                        for tap in range(TAPS):
                            for ft in range(CT):
                                w = cw[:, layer, tap * CT + ft:tap * CT + ft + 1]
                                src = pad[:, ft, tap:tap + SEQ]
                                if tap == 0:
                                    last = dve.tensor_scalar(acc[:, ft, :], src, w, None, ALU.mult)
                                else:
                                    last = dve.scalar_tensor_tensor(out=acc[:, ft, :], in0=src, scalar=w,
                                                                    in1=acc[:, ft, :], op0=ALU.mult, op1=ALU.add)
                            last.then_inc(conv_step, 1)
                            dve.wait_ge(conv_step, step + 2 + tap)
                        for ft in range(CT):
                            dve.tensor_tensor(feat[:, ft, :], feat[:, ft, :], acc[:, ft, :],
                                              ALU.mult).then_inc(y_ready, 1)
                        for ft in range(CT):
                            mix_lo_of(mixT_lo[:, AT + BT + ft, :], feat[:, ft, :], mixT_hi[:, AT + BT + ft, :],
                                      pieces + 4 + ft)
                add_residual(OUT_BANK, lambda q: finished(q, 2 * layer, b + MIX_SLOTS), 8 * layer or None)

            def dense_step(n0, s, rounds):
                it = dict(it=rounds, per=RAW)
                split(n0 + 2, **it)
                split(n0 + 3, **it)
                multiply(n0 + 2 + RAW * rounds, s + 2 * rounds)
                split(n0 + 4, **it)
                dense_lo(s + 2 * rounds)

            def multiply(used, s):
                dve.wait_ge(silu_ready, s + 1)
                dve.wait_ge(hlo_ready, s)
                dve.wait_ge(slots_used, used)
                dve.tensor_tensor(hmul[:, :], pU[:, :], sg[:, :], ALU.mult).then_inc(hmul_ready, 1)

            def dense_lo(s):
                dve.wait_ge(hhi_ready, s + 1)
                dve.tensor_tensor(hT_lo[:, :], hmul[:, :], hT_hi[:, :].bitcast(F32), ALU.subtract).then_inc(hlo_ready, 1)

            def dense():
                norm(1)
                b = DENSE_BASE
                split(b + 1)
                split(b + 2)
                split(b + 3)
                multiply(b + 2, 0)
                dense_lo(0)
                with dve.Fori(0, DENSE_STEPS // 2) as r:
                    for u in range(2):
                        dense_step(b + 2 + 3 * u, 1 + u, r)
                add_residual(pS, lambda q: finished(q, 1, b + DENSE_SLOTS), 4)

            def route():
                norm(3)
                steps = [0]

                def step(*results):
                    for ins in results:
                        steps[0] += 1
                        ins.then_inc(route_step, 1)
                    dve.wait_ge(route_step, steps[0])

                dve.wait_ge(logits_done, 1)
                dve.tensor_copy(lgT, pY0[0:E, 0:SEQ]).then_inc(lgT_ready, 1)
                dve.wait_ge(logits_turned, 1)
                step(dve.tensor_copy(lg, pY1[:, 0:NT * E].rearrange("p (t e) -> p t e", t=NT)))
                step(*[dve.max(top[:, t, :], lg[:, t, :]) for t in range(NT)])
                step(*[dve.max_index(topi[:, t, :], top[:, t, :], lg[:, t, :]) for t in range(NT)])
                dve.tensor_tensor(rt[:, 0, :], top[:, :, 1], top[:, :, 0], ALU.subtract).then_inc(diff_ready, 1)
                step(dve.tensor_copy(topf, topi[:, :, :]))
                step(*[dve.tensor_scalar(oh[:, 2 * t + k, :], iota[:, 0:E], topf[:, t, k:k + 1], None, ALU.is_equal)
                       for t in range(NT) for k in range(TOP_K)])
                oh_t = oh.rearrange("p (t k) e -> p t k e", t=NT)
                dve.tensor_tensor(sel[:, :, :], oh_t[:, :, 0, :], oh_t[:, :, 1, :], ALU.add).then_inc(sel_ready, 1)
                dve.wait_ge(sel_ready, 1)
                step(dve.tensor_copy(tab[:, 0:E, SEL:SEL + NT].rearrange("p e t -> p t e"), sel[:, :, :]))
                dve.wait_ge(exp_ready, 1)
                step(dve.tensor_scalar(rt[:, 3, :], rt[:, 1, :], 1.0, None, ALU.add))
                step(dve.reciprocal(rt[:, 2, :], rt[:, 3, :]))
                step(dve.tensor_tensor(rt[:, 3, :], rt[:, 1, :], rt[:, 2, :], ALU.mult))
                dve.wait_ge(ranks_done, 1)
                step(*[dve.tensor_copy(tab[:, 0:E, RANK + t], ranks[:, 0:E]) for t, ranks in enumerate((pG, pS[0]))])
                for t in range(NT):
                    last = dve.tensor_scalar(pick[:, t, :], iota[:, :], tab[:, 0, RANK + t:RANK + t + 1],
                                             tab[:, 0, SEL + t:SEL + t + 1], ALU.is_equal, ALU.mult)
                last.then_inc(pick_ready, 1)
                step(*[dve.tensor_scalar(oh[:, 2 * t, :], oh[:, 2 * t, :], rt[:, 2, t:t + 1], None, ALU.mult)
                       for t in range(NT)])
                step(*[dve.scalar_tensor_tensor(out=tab[:, 0:E, GATE + t], in0=oh[:, 2 * t + 1, :],
                                                scalar=rt[:, 3, t:t + 1], in1=oh[:, 2 * t, :], op0=ALU.mult,
                                                op1=ALU.add) for t in range(NT)],
                     dve.tensor_copy(tab[:, 0:E, EID], iota[:, 0:E]))
                dve.wait_ge(ranks_done, 2)
                step(dve.tensor_scalar(over[:, 0, :], pY0[:, 0:E], float(P), None, ALU.is_gt))
                step(dve.tensor_tensor_scan(over[:, 1, :], one_row[:, :], over[:, 0, :], 0.0, ALU.mult, ALU.add))
                step(*[dve.scalar_tensor_tensor(out=ohj[:, j, :], in0=over[:, 1, :], scalar=float(j + 1),
                                                in1=over[:, 0, :], op0=ALU.is_equal, op1=ALU.mult)
                       for j in range(OVER)])
                step(*[dve.tensor_tensor(prod[:, j * TAB:(j + 1) * TAB, :],
                                         tab[:, 0:E, :].rearrange("p e c -> p c e"),
                                         ohj[:, j:j + 1, :].to_broadcast([P, TAB, E]), ALU.mult)
                       for j in range(OVER)])
                step(dve.tensor_reduce(tab[:, E:E + OVER, :].rearrange("p e c -> p (e c)"), prod, AX.X, ALU.add))
                step(dve.tensor_scalar(tab[:, E:E + OVER, RANK:RANK + NT], tab[:, E:E + OVER, RANK:RANK + NT],
                                       -float(P), None, ALU.add))
                dve.tensor_copy(steer[0:1, 0:OVER + 1], tab[0:1, E:E + OVER + 1, EID]).then_inc(steer_ready, 1)
                dve.tensor_copy(steer[0:1, OVER + 1:OVER + 2], over[0:1, 1, E - 1:E]).then_inc(steer_ready, 1)
                evacuate_gather(0, halves=[0])
                split(MOE_BASE + 1)
                evacuate_gather(0, halves=[1])
                split(MOE_BASE + 2)

            def evacuate_gather(g, halves=(0, 1)):
                for q in halves:
                    dve.wait_ge(gxhi_ready, 2 * g + q + 1)
                    dve.tensor_tensor(xT_lo[:, 4 * q:4 * q + 4, 0:P],
                                      GATHER_BANK[q][:, :].rearrange("p (k s) -> p k s", k=4),
                                      xT_hi[:, 4 * q:4 * q + 4, 0:P].bitcast(F32), ALU.subtract).then_inc(gxlo_ready, 1)

            def first_slots(it):
                evacuate_gather(it)
                for i in range(SPLIT):
                    split(MOE_BASE + i, it)

            H0 = DENSE_STEPS

            def item(it, ahead):
                B = MOE_BASE

                def hT_low(c):
                    dve.wait_ge(hhi_ready, H0 + c + 1 + CHUNKS * it)
                    dve.tensor_tensor(hT_lo[:, :], pS[0][:, :], hT_hi[:, :].bitcast(F32),
                                      ALU.subtract).then_inc(hlo_ready, 1)

                for c in range(CHUNKS):
                    n0 = chunk_slot(c)
                    if c >= 1:
                        split(B + n0 + 2, it)
                        hT_low(c - 1)
                    for k in range(3, 6):
                        split(B + n0 + k, it)
                    if c >= 1:
                        dve.wait_ge(h_turned, c + CHUNKS * it)
                    multiply(B + n0 + 4 + ITEM * it, H0 + c + CHUNKS * it)
                    if c >= 1:
                        split(B + n0 + 6, it)
                        if ahead or c < CHUNKS - 1:
                            split(B + n0 + 7, it)
                    if c == 3:
                        dve.wait_ge(pick_turned, it + 1)
                        dve.tensor_copy(cur[:, :, :], tab[:, bass.ds(it, 2), :]).then_inc(cur_ready, 1)
                        dve.wait_ge(cur_ready, it + 1)
                        for t in range(NT):
                            last = dve.tensor_scalar(pick[:, t, :], iota[:, :], cur[:, 1, RANK + t:RANK + t + 1],
                                                     cur[:, 1, SEL + t:SEL + t + 1], ALU.is_equal, ALU.mult)
                        last.then_inc(pick_ready, 1)
                hT_low(CHUNKS - 1)
                if not ahead:
                    split(B + ITEM - 1, it)
                if ahead:
                    split(B + ITEM, it)
                    evacuate_gather(it + 1, halves=[0])
                for c in range(2):
                    dve.wait_ge(yhi_ready, c + 1 + 2 * it)
                    dve.tensor_tensor(y_lo[:, 4 * c:4 * c + 4, :], pY[c][:, :].rearrange("p (k s) -> p k s", k=4),
                                      y_hi[:, 4 * c:4 * c + 4, :].bitcast(F32), ALU.subtract).then_inc(ylo_ready, 1)
                if ahead:
                    split(B + ITEM + 1, it)
                    evacuate_gather(it + 1, halves=[1])
                    split(B + ITEM + 2, it)
                dve.wait_ge(res_added, RES_BASE + 4 * it)
                for c in range(2):
                    for t in range(NT):
                        cols = slice(c * BANK, (c + 1) * BANK)
                        dve.wait_ge(scattered, NT * c + t + 1 + 4 * it)
                        dve.scalar_tensor_tensor(out=h[:, t, cols], in0=pS[2 * t + c][:, :],
                                                 scalar=cur[:, 0, GATE + t:GATE + t + 1], in1=h[:, t, cols],
                                                 op0=ALU.mult, op1=ALU.add).then_inc(res_added, 1)

            mix(0)
            dense()
            dve.wait_ge(rwhi_ready, 1)
            dve.tensor_tensor(rw_lo, rw[:, :, :], rw_hi.bitcast(F32), ALU.subtract).then_inc(rwlo_ready, 1)
            mix(1)
            route()
            with dve.Fori(0, E - 1) as it:
                item(it, True)
            item(E - 1, False)
            dve.wait_ge(steer_ready, 2)
            extra = dve.value_load(steer[0:1, OVER + 1:OVER + 2], min_val=0, max_val=OVER)
            with dve.Fori(0, OVER) as j:
                with dve.If(extra > j):
                    first_slots(j + E)
                    item(j + E, False)
            norm(4, turned=False)

        @block.tensor
        def _(pe):
            def product(dst, a_hi, a_lo, b_hi, b_lo, first, last):
                pe.matmul(dst, a_hi, b_hi, start=first, stop=False)
                pe.matmul(dst, a_hi, b_lo, start=False, stop=False)
                return pe.matmul(dst, a_lo, b_hi, start=False, stop=last)

            def token_product(dst, t, k, w_of, n, first, last):
                return product(dst, xT_hi[:, k, t * P:(t + 1) * P], xT_lo[:, k, t * P:(t + 1) * P],
                               w_of(slot_hi(n)), w_of(slot_lo(n)), first, last)

            def feature_tile(dst, n, col, width=2 * P):
                for k in range(KT):
                    last = product(dst, eight_k(slot_hi(n), width)[:, k, col:col + P],
                                   eight_k(slot_lo(n), width)[:, k, col:col + P], xT_hi[:, k, :], xT_lo[:, k, :],
                                   k == 0, k == KT - 1)
                return last

            def keep_clock(bank, count):
                for _ in range(count):
                    pe.matmul(bank[:, 0:P], ident[:, :], ident[:, :], start=True, stop=True)

            def hi_first(dst, w_hi_of, w_lo_of, m):
                for k in range(KT):
                    if k % 4 == 0:
                        pe.wait_ge(xhi_ready, 4 * m + 3 + k // 4)
                    pe.matmul(dst, w_hi_of(k), xT_hi[:, k, :], start=k == 0, stop=False)
                    pe.matmul(dst, w_lo_of(k), xT_hi[:, k, :], start=False, stop=False)

            def lo_last(dst, w_hi_of, m):
                for k in range(KT):
                    if k % 4 == 0:
                        pe.wait_ge(xlo_ready, 4 * m + 3 + k // 4)
                    last = pe.matmul(dst, w_hi_of(k), xT_lo[:, k, :], start=False, stop=k == KT - 1)
                return last

            def turn_normed(m):
                for t in range(NT):
                    for q in range(2):
                        pe.wait_ge(hn_ready, 4 * m + 2 * t + q + 1)
                        for k in range(4):
                            last = pe.transpose(pS[2 * t + q][:, k * P:(k + 1) * P],
                                                hn[:, t, (4 * q + k) * P:(4 * q + k + 1) * P], ident[:, :])
                        last.then_inc(hn_turned, 1)

            def mix(layer):
                b = MIX_BASE[layer]
                f = b + MIX_IN_TOKEN
                pieces = (3 + CT) * layer
                if layer > 0:
                    keep_clock(pG, 9)
                turn_normed(2 * layer)
                for i in range(MIX_IN_TOKEN):
                    n, j, kh = b + i, i // 2, i % 2
                    if n > 0:
                        pe.wait_ge(lo_ready, n + 1)
                    for t in range(NT):
                        pe.wait_ge(xlo_ready, 8 * layer + 2 * t + kh + 1)
                        if n == 0 and t == 0:
                            pe.wait_ge(hi_ready, 1)
                            for k in range(4):
                                for x_part in (xT_hi, xT_lo):
                                    pe.matmul(pS[0][:, :], x_part[:, k, 0:P], four_k(slot_hi(0))[:, k, :],
                                              start=k == 0 and x_part is xT_hi, stop=False)
                            pe.wait_ge(lo_ready, 1)
                            for k in range(4):
                                pe.matmul(pS[0][:, :], xT_hi[:, k, 0:P], four_k(slot_lo(0))[:, k, :],
                                          start=False, stop=False)
                            continue
                        for k in range(4):
                            last = token_product(pS[2 * j + t][:, :], t, 4 * kh + k, lambda s: four_k(s)[:, k, :], n,
                                                 kh == 0 and k == 0, kh == 1 and k == 3)
                    last.then_inc(slots_used, 1)
                    if layer == 0 and i == 2:
                        pe.wait_ge(ws_loaded, 16)
                        for q in range(3):
                            for k in range(4):
                                last = pe.transpose(banks[q][:, k * P:(k + 1) * P], ws_raw[:, 4 * q + k, :],
                                                    ident[:, :])
                            last.then_inc(ws_turned, 1)
                for i in range(MIX_IN_FEAT):
                    n = f + i
                    tiles = min(2, FEAT_TILES - 2 * i)
                    pe.wait_ge(lo_ready, n + 1)
                    if i == 0:
                        pe.wait_ge(wsT_ready, 1)
                    if i == 4:
                        pe.wait_ge(feat_ready, MIX_IN_FEAT * layer + 1)
                    for ft in range(tiles):
                        last = feature_tile(FEAT_BANK[i][:, ft * SEQ:(ft + 1) * SEQ], n, ft * P, tiles * P)
                    last.then_inc(slots_used, 1)
                    if i == 0:
                        pe.wait_ge(dft_loaded, 32)
                        pe.wait_ge(a_ready, 2 * layer + 2)
                        pe.wait_ge(uv_ready, 4 * layer + 2)
                        for g in range(AT):
                            for t in range(NT):
                                last = pe.matmul(pS[g][:, :], a_sb[:, t, g * P:(g + 1) * P], cs[:, t, :],
                                                 start=t == 0, stop=t == NT - 1)
                            last.then_inc(dft1_done, 1)
                    if i == 1:
                        pe.wait_ge(dft1_ready, AT * (layer + 1))
                        for g in range(AT):
                            for part in range(2):
                                last = pe.matmul(pS[0][:, g * SEQ:(g + 1) * SEQ], bd[:, part, :],
                                                 dft1[g][:, part * SEQ:(part + 1) * SEQ],
                                                 start=part == 0, stop=part == 1)
                        last.then_inc(dft2_done, 1)
                    if i == 2:
                        pe.wait_ge(uv_ready, 4 * layer + 4)
                        for t in range(NT):
                            pe.wait_ge(vn_ready, 2 * (NT * layer + t + 1))
                            for hd in range(HEADS_B):
                                last = pe.matmul(pS[2 + t][:, hd * HEAD:(hd + 1) * HEAD],
                                                 wsT[:, layer * HEADS_B + hd, :],
                                                 uv_t[:, t, W_B + hd * HEAD:W_B + (hd + 1) * HEAD],
                                                 start=True, stop=True)
                            last.then_inc(z_done, 1)
                    if i == 3:
                        pe.wait_ge(g_ready, NT * (layer + 1))
                        for k in range(BT):
                            if k == 2:
                                pe.wait_ge(mixlo_ready, pieces + 1)
                            for t in range(NT):
                                bank, col = (pS[1], k * SEQ) if k < 2 else (pS[0], 0)
                                last = pe.transpose(bank[:, col + t * P:col + (t + 1) * P],
                                                    uv_t[:, t, k * P:(k + 1) * P], ident[:, :])
                            if k >= 1:
                                last.then_inc(g_turned, 1)
                pe.wait_ge(feat_ready, MIX_IN_FEAT * layer + 3)
                for i in range(MIX_OUT):
                    n = b + MIX_IN + i
                    pe.wait_ge(lo_ready, n + 1)
                    pe.wait_ge(mixlo_ready, pieces + (1, 2, 4, 6)[i])
                    for kk, t in TILE_LAST if i == MIX_OUT - 1 else K_LAST:
                        k = 2 * i + kk
                        rows = slice(t * P, (t + 1) * P)
                        for c in range(2):
                            cols = slice(c * BANK, (c + 1) * BANK)
                            last = product(OUT_BANK[2 * t + c][:, :], mixT_hi[:, k, rows], mixT_lo[:, k, rows],
                                           two_k(slot_hi(n))[:, kk, cols], two_k(slot_lo(n))[:, kk, cols],
                                           k == 0, k == KT - 1)
                        if i == MIX_OUT - 1 and kk == 1 and t == 0:
                            last.then_inc(first_tile_done, 1)
                    last.then_inc(slots_used, 1)

            def up_slot(n, dst, rounds):
                pe.wait_ge(lo_ready, n + 1 + RAW * rounds)
                for ft in range(2):
                    last = feature_tile(dst[:, ft * SEQ:(ft + 1) * SEQ], n, ft * P)
                last.then_inc(slots_used, 1)

            def down_slot(n, s, rounds, first=False, final=False):
                pe.wait_ge(lo_ready, n + 1 + RAW * rounds)
                pe.wait_ge(hlo_ready, s + 1 + 2 * rounds)
                for ft, t in TILE_LAST if final else K_LAST:
                    rows = slice(ft * SEQ + t * P, ft * SEQ + (t + 1) * P)
                    for c in range(2):
                        cols = slice(c * BANK, (c + 1) * BANK)
                        last = product(pS[2 * t + c][:, :], hT_hi[:, rows], hT_lo[:, rows],
                                       two_k(slot_hi(n))[:, ft, cols], two_k(slot_lo(n))[:, ft, cols],
                                       first and ft == 0, final and ft == 1)
                    if final and ft == 1 and t == 0:
                        last.then_inc(first_tile_done, 1)
                last.then_inc(slots_used, 1)

            def dense_step(n0, s, rounds, first=False):
                pe.wait_ge(silu_ready, s + 2 * rounds)
                up_slot(n0, pG, rounds)
                pe.wait_ge(hmul_ready, s + 2 * rounds)
                up_slot(n0 + 1, pU, rounds)
                down_slot(n0 + 2, s - 1, rounds, first=first)

            def dense():
                b = DENSE_BASE
                keep_clock(pG, 9)
                turn_normed(1)
                pe.wait_ge(lo_ready, b + 1)
                for ft in range(2):
                    hi_first(pG[:, ft * SEQ:(ft + 1) * SEQ],
                             lambda k: eight_k(slot_hi(b))[:, k, ft * P:(ft + 1) * P],
                             lambda k: eight_k(slot_lo(b))[:, k, ft * P:(ft + 1) * P], 1)
                    last = lo_last(pG[:, ft * SEQ:(ft + 1) * SEQ],
                                   lambda k: eight_k(slot_hi(b))[:, k, ft * P:(ft + 1) * P], 1)
                last.then_inc(slots_used, 1)
                up_slot(b + 1, pU, 0)
                for u in range(2):
                    dense_step(b + 2 + 3 * u, 1 + u, 0, first=u == 0)
                with pe.Fori(1, DENSE_STEPS // 2) as r:
                    for u in range(2):
                        dense_step(b + 2 + 3 * u, 1 + u, r)
                down_slot(b + DENSE_SLOTS - 1, DENSE_STEPS - 1, 0, final=True)

            def gather(count, halves=(0, 1)):
                pe.wait_ge(pick_ready, count)
                for q in halves:
                    for k in range(4):
                        cols = slice((4 * q + k) * P, (4 * q + k + 1) * P)
                        for t in range(NT):
                            last = pe.matmul(GATHER_BANK[q][:, k * P:(k + 1) * P], hn[:, t, cols], pick[:, t, :],
                                             start=t == 0, stop=t == NT - 1)
                    last.then_inc(gathered, 1)

            def route():
                keep_clock(pG, 12)
                turn_normed(3)
                pe.wait_ge(rwlo_ready, 1)
                hi_first(pY0[0:E, 0:SEQ], lambda k: rw_hi[:, k, :], lambda k: rw_lo[:, k, :], 3)
                lo_last(pY0[0:E, 0:SEQ], lambda k: rw_hi[:, k, :], 3).then_inc(logits_done, 1)
                keep_clock(pG, 3)
                pe.wait_ge(lgT_ready, 1)
                for t in range(NT):
                    last = pe.transpose(pY1[:, t * E:(t + 1) * E], lgT[:, t * P:(t + 1) * P], ident[0:E, 0:E])
                last.then_inc(logits_turned, 1)
                keep_clock(pG, 9)
                pe.wait_ge(sel_ready, 1)
                pe.matmul(pG[:, 0:E], before[:, :], sel[:, 0, :], start=True, stop=True)
                for dst in (pS[0], pY0):
                    pe.matmul(dst[:, 0:E], ones[:, :], sel[:, 0, :], start=True, stop=False)
                for dst, own in ((pS[0], before), (pY0, ones)):
                    pe.matmul(dst[:, 0:E], own[:, :], sel[:, 1, :], start=False, stop=True).then_inc(ranks_done, 1)
                keep_clock(pU, 4)
                gather(1)

            H0 = DENSE_STEPS

            def item(it, ahead):
                B = MOE_BASE

                def up_half(i, k0, dst):
                    pe.wait_ge(lo_ready, B + i + 1 + ITEM * it)
                    for k in range(4):
                        last = token_product(dst[:, :], 0, k0 + k, lambda s: four_k(s)[:, k, :], B + i,
                                             k0 + k == 0, k0 + k == KT - 1)
                    last.then_inc(slots_used, 1)

                def turn_h(c):
                    pe.wait_ge(hmul_ready, H0 + c + 1 + CHUNKS * it)
                    if c == 0:
                        pe.wait_ge(res_added, RES_BASE + 4 * it)
                    else:
                        pe.wait_ge(hlo_ready, H0 + c + CHUNKS * it)
                    for k in range(4):
                        last = pe.transpose(pS[0][:, k * P:(k + 1) * P], hmul[:, k * P:(k + 1) * P], ident[:, :])
                    last.then_inc(h_turned, 1)

                def down(i, c):
                    pe.wait_ge(hlo_ready, H0 + c + 1 + CHUNKS * it)
                    for half in range(2):
                        n = B + i + half
                        pe.wait_ge(lo_ready, n + 1 + ITEM * it)
                        final = c == CHUNKS - 1 and half == 1
                        for kk, d in TILE_LAST if final else K_LAST:
                            k = 2 * half + kk
                            cols = slice(d * BANK, (d + 1) * BANK)
                            last = product(pY[d][:, :], hT_hi[:, k * P:(k + 1) * P], hT_lo[:, k * P:(k + 1) * P],
                                           two_k(slot_hi(n))[:, kk, cols], two_k(slot_lo(n))[:, kk, cols],
                                           c == 0 and k == 0, c == CHUNKS - 1 and k == 3)
                            if final and kk == 1 and d == 0:
                                last.then_inc(y_half_done, 1)
                        last.then_inc(slots_used, 1)

                for c in range(CHUNKS):
                    n0 = chunk_slot(c)
                    if c == 0:
                        pe.wait_ge(gxlo_ready, 2 * it + 1)
                    pe.wait_ge(silu_ready, H0 + c + CHUNKS * it)
                    up_half(n0, 0, pG)
                    if c >= 1:
                        turn_h(c - 1)
                    if c == 1:
                        for t in range(NT):
                            last = pe.transpose(pS[1][:, t * P:(t + 1) * P], pick[:, t, :], ident[:, :])
                        last.then_inc(pick_turned, 1)
                    if c == 0:
                        pe.wait_ge(gxlo_ready, 2 * it + 2)
                    up_half(n0 + 1, 4, pG)
                    pe.wait_ge(hmul_ready, H0 + c + CHUNKS * it)
                    up_half(n0 + 2, 0, pU)
                    up_half(n0 + 3, 4, pU)
                    if c >= 1:
                        down(n0 + 4, c - 1)
                turn_h(CHUNKS - 1)
                pe.wait_ge(pickT_ready, it + 1)
                if ahead:
                    gather(it + 2, halves=[0])
                down(chunk_slot(CHUNKS), CHUNKS - 1)
                if ahead:
                    gather(it + 2, halves=[1])
                for c in range(2):
                    pe.wait_ge(ylo_ready, c + 1 + 2 * it)
                    for t in range(NT):
                        if ahead and (t, c) == (0, 1):
                            pe.wait_ge(gxlo_ready, 2 * it + 3)
                        pe.matmul(pS[2 * t + c][:, :], pickT[:, t, :], y_hi[:, 4 * c:4 * c + 4, :],
                                  start=True, stop=False)
                        pe.matmul(pS[2 * t + c][:, :], pickT[:, t, :], y_lo[:, 4 * c:4 * c + 4, :],
                                  start=False, stop=True).then_inc(scattered, 1)

            pe.wait_ge(masks_ready, 1)
            keep_clock(pU, 16)
            mix(0)
            dense()
            mix(1)
            route()
            with pe.Fori(0, E - 1) as it:
                item(it, True)
            item(E - 1, False)
            pe.wait_ge(steer_ready, 2)
            extra = pe.value_load(steer[0:1, OVER + 1:OVER + 2], min_val=0, max_val=OVER)
            with pe.Fori(0, OVER) as j:
                with pe.If(extra > j):
                    pe.wait_ge(res_added, RES_BASE + 4 * (j + E))
                    gather(j + E + 1)
                    item(j + E, False)


def dft_tables(seq, head, per_tile):
    s = np.arange(seq)
    angle = 2 * np.pi * (np.outer(s, s) % seq) / seq
    over_seq = np.concatenate([np.cos(angle), np.sin(angle)], axis=1).astype(np.float32)
    d = np.arange(head)
    angle = 2 * np.pi * (np.outer(d, d) % head) / head
    scale = 1.0 / np.sqrt(seq * head)
    over_head = np.stack([np.kron(np.eye(per_tile), np.cos(angle) * scale),
                          np.kron(np.eye(per_tile), -np.sin(angle) * scale)]).astype(np.float32)
    return over_seq, over_head


_INS = ['x', 'norm_mix_g', 'w_in', 'vnorm_g', 'vnorm_b', 'w_spatial', 'b_spatial', 'conv_w', 'w_out',
        'norm_ffn_g', 'dense_w_gate', 'dense_w_up', 'dense_w_down', 'router_w',
        'moe_w_gate', 'moe_w_up', 'moe_w_down', 'norm_final_g']


def kernel(**inputs):
    import numpy as _np
    import concourse.bacc as _bacc
    from concourse import mybir as _mybir
    from concourse.bass_utils import run_bass_kernel_spmd as _run

    nc = _bacc.Bacc("TRN2", target_bir_lowering=False, num_devices=1)
    arrays, args = {}, []
    data = {name: _np.ascontiguousarray(inputs[name]) for name in _INS}
    seq = data['x'].shape[1]
    w_a = data['w_in'].shape[2] - 2 * data['vnorm_g'].shape[1] - 3 * data['conv_w'].shape[2]
    head = w_a // GROUPS_A
    data['dft_seq'], data['dft_head'] = dft_tables(seq, head, P // head)
    for name, a in data.items():
        arrays[f"in_{name}_dram"] = a
        args.append(nc.dram_tensor(f"in_{name}_dram", a.shape, _mybir.dt.from_np(a.dtype), kind="ExternalInput").ap())
    shape = data['x'].shape
    args.append(nc.dram_tensor("out_0_dram", shape, _mybir.dt.float32, kind="ExternalOutput").ap())
    hybrid_encoder(nc, *args)
    r = _run(nc, [arrays], core_ids=[0])
    return r.results[0]["out_0_dram"]
```
